# Optimizing a Trainium2 kernel written in Bass

```python
import math
import jax, jax.numpy as jnp
from jax import lax
import numpy as np

'''One inference step of a hybrid autoregressive decoder trunk (DEPTH layers), prompt and sample groups sharing weights.

Each layer is a post-LN (DeepNorm) macaron block with adaLN conditioning:
  x <- LN(alpha*x + 1/2 * gate1 * SwiGLU1(mod1(x)))
  x <- LN(alpha*x + gate2 * W_out [ A(mod2(x)) | B(mod2(x)) ])   (parallel head groups, one combined input projection)
  x <- LN(alpha*x + 1/2 * gate3 * SwiGLU2(mod3(x)))
A: dilated sliding-window attention, 8 heads, (window,dilation) branches (128,1),(512,4),(2048,16), keys gathered by
   stride, branch outputs merged weighted by softmax denominators; B: sliding-window (128) GQA, 8 q heads / 2 kv heads,
   learned per-head sinks. Both add a T5 relative-position bias (32 causal log buckets, table shared by all layers).

Inputs: x_prompt (BATCH,SEQ,D_MODEL), x_sample (DEC_BATCH,DEC_SEQ,D_MODEL),
  cache_a_k/v (DEPTH,DEC_BATCH,min(2048,PAST_LEN),8,64), cache_b_k/v (DEPTH,DEC_BATCH,min(128,PAST_LEN),2,64)
  (contiguous window buffers holding positions PAST_LEN-rows..PAST_LEN-1), c_prompt (BATCH,D_MODEL),
  c_sample (DEC_BATCH,D_MODEL), then weights.
Returns (y_prompt (BATCH,SEQ,D), y_sample (DEC_BATCH,DEC_SEQ,D),
  new_a_k_prompt, new_a_v_prompt (DEPTH,BATCH,min(2048,SEQ),8,64),
  new_b_k_prompt, new_b_v_prompt (DEPTH,BATCH,min(128,SEQ),2,64),
  new_a_k_sample, new_a_v_sample (DEPTH,DEC_BATCH,DEC_SEQ,8,64),
  new_b_k_sample, new_b_v_sample (DEPTH,DEC_BATCH,DEC_SEQ,2,64)).
'''

D_MODEL = 1024
BATCH = 1
SEQ = 1024
DEPTH = 1
DEC_BATCH = 8
DEC_SEQ = 1
PAST_LEN = 2048
PAGE_SIZE = 128

HEAD_DIM = 64
MIX_WIDTH = D_MODEL
N_HEADS_A = MIX_WIDTH // 2 // HEAD_DIM
N_HEADS_B = MIX_WIDTH // 2 // HEAD_DIM
N_KV_B = N_HEADS_B // 4
GQA_GROUP = N_HEADS_B // N_KV_B
A_PATTERNS = ((128, 1), (512, 4), (2048, 16))
A_WINDOW_MAX = 2048
B_WINDOW = 128
BLK = 128
D_FF = 2816
NUM_BUCKETS = 32
MAX_DISTANCE = 2048
N_HEADS_TOTAL = N_HEADS_A + N_HEADS_B
ALPHA = (2 * DEPTH) ** 0.25
BETA = (8 * DEPTH) ** -0.25
LN_EPS = 1e-5
NEG = -1e30
SCALE = HEAD_DIM ** -0.5
PROJ_COLS = 3 * N_HEADS_A * HEAD_DIM + N_HEADS_B * HEAD_DIM + 2 * N_KV_B * HEAD_DIM

kernel_name = "hymba_dilated_swa_sink_macaron_deepnorm_step"

def t5_bucket(n):
    max_exact = NUM_BUCKETS // 2
    nf = jnp.maximum(n, 1).astype(jnp.float32)
    large = max_exact + (jnp.log(nf / max_exact) / math.log(MAX_DISTANCE / max_exact)
                         * (NUM_BUCKETS - max_exact)).astype(jnp.int32)
    return jnp.where(n < max_exact, n, jnp.minimum(large, NUM_BUCKETS - 1))

def layer_norm(x, g, b):
    xf = x.astype(jnp.float32)
    mu = jnp.mean(xf, -1, keepdims=True)
    var = jnp.mean(jnp.square(xf - mu), -1, keepdims=True)
    return ((xf - mu) * lax.rsqrt(var + LN_EPS) * g + b).astype(x.dtype)

def swiglu(h, wg, wu, wd):
    return (jax.nn.silu(h @ wg) * (h @ wu)) @ wd

def softmax_parts(s, sink):
    m = jnp.max(s, -1, keepdims=True)
    if sink is not None:
        m = jnp.maximum(m, sink)
    p = jnp.exp(s - m)
    den = jnp.sum(p, -1, keepdims=True)
    if sink is not None:
        den = den + jnp.exp(sink - m)
    return p, den, m

def banded_attn(q, k, v, bias_heads, step, win_units, sink):
    N, L, Hk, G, hd = q.shape
    nb = L // BLK
    qb = q.reshape(N, nb, BLK, Hk, G, hd)
    kb = k.reshape(N, nb, BLK, Hk, hd)
    vb = v.reshape(N, nb, BLK, Hk, hd)
    pad = ((0, 0), (1, 0), (0, 0), (0, 0), (0, 0))
    kk = jnp.concatenate([jnp.pad(kb, pad)[:, :-1], kb], axis=2)
    vv = jnp.concatenate([jnp.pad(vb, pad)[:, :-1], vb], axis=2)
    dist = jnp.arange(BLK)[:, None] + BLK - jnp.arange(2 * BLK)[None, :]
    valid = (dist >= 0) & (dist <= win_units)
    bias = bias_heads[t5_bucket(jnp.maximum(dist, 0) * step)].astype(jnp.float32)
    bias = jnp.where(valid[..., None], bias, NEG)
    bias = bias.transpose(2, 0, 1).reshape(Hk, G, BLK, 2 * BLK)
    first = (jnp.arange(nb)[:, None] == 0) & (jnp.arange(2 * BLK)[None, :] < BLK)
    s = jnp.einsum('nbqhgd,nbkhd->nbhgqk', qb, kk).astype(jnp.float32) * SCALE + bias
    s = jnp.where(first[None, :, None, None, None, :], NEG, s)
    sink_b = None if sink is None else sink.astype(jnp.float32).reshape(1, 1, Hk, G, 1, 1)
    p, den, m = softmax_parts(s, sink_b)
    o = jnp.einsum('nbhgqk,nbkhd->nbqhgd', p, vv.astype(jnp.float32))
    o = o / den[..., 0].transpose(0, 1, 4, 2, 3)[..., None]
    lse = (m + jnp.log(den))[..., 0].transpose(0, 1, 4, 2, 3)
    return o.reshape(N, L, Hk, G, hd), lse.reshape(N, L, Hk, G)

def gathered_attn(q, kfull, vfull, base, bias_heads, step, win_units, sink):
    N, T, Hk, G, hd = q.shape
    i = jnp.arange(win_units + 1)
    idx = base + jnp.arange(T)[:, None] - step * i[None, :]
    valid = idx >= 0
    idxc = jnp.maximum(idx, 0)
    kg = kfull[:, idxc]
    vg = vfull[:, idxc]
    bias = bias_heads[t5_bucket(i * step)].astype(jnp.float32).T.reshape(Hk, G, win_units + 1)
    s = jnp.einsum('nthgd,ntkhd->nthgk', q, kg).astype(jnp.float32) * SCALE + bias
    s = jnp.where(valid[None, :, None, None, :], s, NEG)
    sink_b = None if sink is None else sink.astype(jnp.float32).reshape(1, 1, Hk, G, 1)
    p, den, m = softmax_parts(s, sink_b)
    o = jnp.einsum('nthgk,ntkhd->nthgd', p, vg.astype(jnp.float32)) / den
    return o, (m + jnp.log(den))[..., 0]

def split_proj(h, w_in):
    na = N_HEADS_A * HEAD_DIM
    nq = N_HEADS_B * HEAD_DIM
    nkv = N_KV_B * HEAD_DIM
    pre = h.shape[:-1]
    proj = h @ w_in
    qa, ka, va, qb, kb, vb = jnp.split(proj, [na, 2 * na, 3 * na, 3 * na + nq, 3 * na + nq + nkv], axis=-1)
    return (qa.reshape(*pre, N_HEADS_A, HEAD_DIM), ka.reshape(*pre, N_HEADS_A, HEAD_DIM),
            va.reshape(*pre, N_HEADS_A, HEAD_DIM), qb.reshape(*pre, N_KV_B, GQA_GROUP, HEAD_DIM),
            kb.reshape(*pre, N_KV_B, HEAD_DIM), vb.reshape(*pre, N_KV_B, HEAD_DIM))

def merge_branches(outs, lses):
    w = jax.nn.softmax(jnp.stack(lses), axis=0)
    return jnp.einsum('rbsh,rbshd->bshd', w, jnp.stack(outs))

def mixer_prompt(h, w_in, w_out, sinks, rel_bias):
    Bn, S, _ = h.shape
    qa, ka, va, qb, kb, vb = split_proj(h, w_in)
    outs, lses = [], []
    for window, dil in A_PATTERNS:
        L = S // dil
        Lp = -(-L // BLK) * BLK

        def to_res(t):
            t = t.reshape(Bn, L, dil, N_HEADS_A, HEAD_DIM).transpose(0, 2, 1, 3, 4)
            t = t.reshape(Bn * dil, L, N_HEADS_A, HEAD_DIM)
            return jnp.pad(t, ((0, 0), (0, Lp - L), (0, 0), (0, 0)))

        o, lse = banded_attn(to_res(qa)[:, :, :, None, :], to_res(ka), to_res(va),
                             rel_bias[:, :N_HEADS_A], dil, window // dil, None)
        o = o[:, :L, :, 0].reshape(Bn, dil, L, N_HEADS_A, HEAD_DIM).transpose(0, 2, 1, 3, 4)
        lse = lse[:, :L, :, 0].reshape(Bn, dil, L, N_HEADS_A).transpose(0, 2, 1, 3)
        outs.append(o.reshape(Bn, S, N_HEADS_A, HEAD_DIM))
        lses.append(lse.reshape(Bn, S, N_HEADS_A))
    oa = merge_branches(outs, lses)
    ob, _ = banded_attn(qb, kb, vb, rel_bias[:, N_HEADS_A:], 1, B_WINDOW, sinks)
    mixed = jnp.concatenate([oa.reshape(Bn, S, -1), ob.reshape(Bn, S, -1)], -1).astype(h.dtype)
    ra = min(A_WINDOW_MAX, S)
    rb = min(B_WINDOW, S)
    return mixed @ w_out, ka[:, S - ra:], va[:, S - ra:], kb[:, S - rb:], vb[:, S - rb:]

def mixer_sample(h, ca_k, ca_v, cb_k, cb_v, w_in, w_out, sinks, rel_bias):
    Bn, T, _ = h.shape
    qa, ka, va, qb, kb, vb = split_proj(h, w_in)
    kfa = jnp.concatenate([ca_k, ka.astype(ca_k.dtype)], 1)
    vfa = jnp.concatenate([ca_v, va.astype(ca_v.dtype)], 1)
    outs, lses = [], []
    for window, dil in A_PATTERNS:
        o, lse = gathered_attn(qa[:, :, :, None, :], kfa, vfa, ca_k.shape[1],
                               rel_bias[:, :N_HEADS_A], dil, window // dil, None)
        outs.append(o[:, :, :, 0])
        lses.append(lse[:, :, :, 0])
    oa = merge_branches(outs, lses)
    kfb = jnp.concatenate([cb_k, kb.astype(cb_k.dtype)], 1)
    vfb = jnp.concatenate([cb_v, vb.astype(cb_v.dtype)], 1)
    ob, _ = gathered_attn(qb, kfb, vfb, cb_k.shape[1], rel_bias[:, N_HEADS_A:], 1, B_WINDOW, sinks)
    mixed = jnp.concatenate([oa.reshape(Bn, T, -1), ob.reshape(Bn, T, -1)], -1).astype(h.dtype)
    return mixed @ w_out, ka, va, kb, vb

def trunk(x, c, mixer, w_ada, b_ada, ffn1_wg, ffn1_wu, ffn1_wd, ffn2_wg, ffn2_wu, ffn2_wd, ln_g, ln_b):
    ak, av, bk, bv = [], [], [], []
    for l in range(DEPTH):
        mod = (jax.nn.silu(c) @ w_ada[l] + b_ada[l]).reshape(c.shape[0], 9, 1, D_MODEL)
        h = x * (1 + mod[:, 1]) + mod[:, 0]
        x = layer_norm(ALPHA * x + 0.5 * mod[:, 2] * swiglu(h, ffn1_wg[l], ffn1_wu[l], ffn1_wd[l]),
                       ln_g[l, 0], ln_b[l, 0])
        h = x * (1 + mod[:, 4]) + mod[:, 3]
        out, k_a, v_a, k_b, v_b = mixer(l, h)
        x = layer_norm(ALPHA * x + mod[:, 5] * out, ln_g[l, 1], ln_b[l, 1])
        h = x * (1 + mod[:, 7]) + mod[:, 6]
        x = layer_norm(ALPHA * x + 0.5 * mod[:, 8] * swiglu(h, ffn2_wg[l], ffn2_wu[l], ffn2_wd[l]),
                       ln_g[l, 2], ln_b[l, 2])
        ak.append(k_a); av.append(v_a); bk.append(k_b); bv.append(v_b)
    return x, jnp.stack(ak), jnp.stack(av), jnp.stack(bk), jnp.stack(bv)

def setup_inputs(seed: int = 0) -> dict:
    key = jax.random.key(seed)
    ks = jax.random.split(key, 24)

    def nrm(k, shape, s):
        return jax.random.normal(k, shape, jnp.float32) * s

    a_rows = min(A_WINDOW_MAX, PAST_LEN)
    b_rows = min(B_WINDOW, PAST_LEN)
    na = N_HEADS_A * HEAD_DIM
    nq = N_HEADS_B * HEAD_DIM
    nkv = N_KV_B * HEAD_DIM
    col_scale = jnp.concatenate([jnp.ones((2 * na,), jnp.float32), jnp.full((na,), BETA, jnp.float32),
                                 jnp.ones((nq + nkv,), jnp.float32), jnp.full((nkv,), BETA, jnp.float32)])
    return {
        "x_prompt": nrm(ks[0], (BATCH, SEQ, D_MODEL), 1.0),
        "x_sample": nrm(ks[1], (DEC_BATCH, DEC_SEQ, D_MODEL), 1.0),
        "cache_a_k": nrm(ks[2], (DEPTH, DEC_BATCH, a_rows, N_HEADS_A, HEAD_DIM), 1.0),
        "cache_a_v": nrm(ks[3], (DEPTH, DEC_BATCH, a_rows, N_HEADS_A, HEAD_DIM), BETA),
        "cache_b_k": nrm(ks[4], (DEPTH, DEC_BATCH, b_rows, N_KV_B, HEAD_DIM), 1.0),
        "cache_b_v": nrm(ks[5], (DEPTH, DEC_BATCH, b_rows, N_KV_B, HEAD_DIM), BETA),
        "c_prompt": nrm(ks[6], (BATCH, D_MODEL), 1.0),
        "c_sample": nrm(ks[7], (DEC_BATCH, D_MODEL), 1.0),
        "rel_bias": nrm(ks[8], (NUM_BUCKETS, N_HEADS_TOTAL), 0.5),
        "w_ada": nrm(ks[9], (DEPTH, D_MODEL, 9 * D_MODEL), 0.5 * D_MODEL ** -0.5),
        "b_ada": nrm(ks[10], (DEPTH, 9 * D_MODEL), 0.02),
        "ffn1_wg": nrm(ks[11], (DEPTH, D_MODEL, D_FF), D_MODEL ** -0.5),
        "ffn1_wu": nrm(ks[12], (DEPTH, D_MODEL, D_FF), D_MODEL ** -0.5),
        "ffn1_wd": nrm(ks[13], (DEPTH, D_FF, D_MODEL), BETA * D_FF ** -0.5),
        "w_in": nrm(ks[14], (DEPTH, D_MODEL, PROJ_COLS), D_MODEL ** -0.5) * col_scale,
        "w_out": nrm(ks[15], (DEPTH, MIX_WIDTH, D_MODEL), BETA * MIX_WIDTH ** -0.5),
        "sinks": nrm(ks[16], (DEPTH, N_HEADS_B), 0.5),
        "ffn2_wg": nrm(ks[17], (DEPTH, D_MODEL, D_FF), D_MODEL ** -0.5),
        "ffn2_wu": nrm(ks[18], (DEPTH, D_MODEL, D_FF), D_MODEL ** -0.5),
        "ffn2_wd": nrm(ks[19], (DEPTH, D_FF, D_MODEL), BETA * D_FF ** -0.5),
        "ln_g": 1.0 + nrm(ks[20], (DEPTH, 3, D_MODEL), 0.05),
        "ln_b": nrm(ks[21], (DEPTH, 3, D_MODEL), 0.05),
    }

def reference(x_prompt, x_sample, cache_a_k, cache_a_v, cache_b_k, cache_b_v, c_prompt, c_sample,
              rel_bias, w_ada, b_ada, ffn1_wg, ffn1_wu, ffn1_wd, w_in, w_out, sinks,
              ffn2_wg, ffn2_wu, ffn2_wd, ln_g, ln_b):
    def mix_p(l, h):
        return mixer_prompt(h, w_in[l], w_out[l], sinks[l], rel_bias)

    def mix_s(l, h):
        return mixer_sample(h, cache_a_k[l], cache_a_v[l], cache_b_k[l], cache_b_v[l],
                            w_in[l], w_out[l], sinks[l], rel_bias)

    y_prompt, pak, pav, pbk, pbv = trunk(x_prompt, c_prompt, mix_p, w_ada, b_ada, ffn1_wg, ffn1_wu, ffn1_wd,
                                         ffn2_wg, ffn2_wu, ffn2_wd, ln_g, ln_b)
    y_sample, sak, sav, sbk, sbv = trunk(x_sample, c_sample, mix_s, w_ada, b_ada, ffn1_wg, ffn1_wu, ffn1_wd,
                                         ffn2_wg, ffn2_wu, ffn2_wd, ln_g, ln_b)
    return (y_prompt, y_sample, pak, pav, pbk, pbv, sak, sav, sbk, sbv)


_drawn_inputs = setup_inputs


def setup_inputs(seed=0):
    import zlib

    import numpy as np

    out = dict(_drawn_inputs(seed))
    spreads = {}
    factors = {'cache_a_k': 8.0,
     'cache_a_v': 7.274,
     'cache_b_k': 7.281,
     'cache_b_v': 5.932,
     'rel_bias': 8.0,
     'sinks': 64.0}
    for name, (base, spread) in spreads.items():
        noise = np.random.default_rng([zlib.crc32(name.encode()), seed]).standard_normal(out[name].shape)
        drawn = base * np.exp(spread * noise) if base else spread * noise
        out[name] = __import__('jax').numpy.asarray(drawn.astype(out[name].dtype))
    for name, factor in factors.items():
        out[name] = (out[name] * factor).astype(out[name].dtype)
    return out
```

```python
import math
from contextlib import ExitStack

import numpy as np

import concourse.bass as bass
from concourse import mybir

P = 128
D = 1024
KT = D // P
TP = 1024
NS = 8
T = TP + NS
TB = TP // P
NG = 3
TG = T // NG
PG = TG - NS
FF = 2816
FT = FF // P
CH = FT // 2
HD = 64
NH = 8
PT = 18
TQA, TKA, TVA, TQB, TKB, TVB = 0, 4, 8, 12, 16, 17
MODS = 9
MT = MODS * KT
NC1 = 1 + NS
ALPHA = 2.0 ** 0.25
EPS = 1e-5
NEG = -1e30
UNIT_D = NG * KT

F32 = mybir.dt.float32
F32R = mybir.dt.float32r
ALU = mybir.AluOpType
ACT = mybir.ActivationFunctionType
AXX = mybir.AxisListType.X


class Arena:

    def __init__(self, nc):
        self.nc, self.base = nc, (nc.sbuf_base + 31) // 32 * 32

    def at(self, name, shape, dtype, offset):
        size = 4 * int(np.prod(shape[1:]))
        assert offset % 32 == 0 and self.base + offset + size <= self.nc.sbuf_usable_end, (name, offset, size)
        return self.nc.alloc_sbuf_tensor_at(name, shape, dtype, offset=self.base + offset)


def up32(n):
    return (n + 31) // 32 * 32


class Numbers:

    def __init__(self, steps):
        self.of = {s: n + 1 for n, s in enumerate(steps)}
        self.total = len(self.of)

    def __getitem__(self, step):
        return self.of[step]

OUTPUTS = [("y_prompt", (1, TP, D)), ("y_sample", (NS, 1, D)),
           ("ak_prompt", (1, 1, TP, NH, HD)), ("av_prompt", (1, 1, TP, NH, HD)),
           ("bk_prompt", (1, 1, P, 2, HD)), ("bv_prompt", (1, 1, P, 2, HD)),
           ("ak_sample", (1, NS, 1, NH, HD)), ("av_sample", (1, NS, 1, NH, HD)),
           ("bk_sample", (1, NS, 1, 2, HD)), ("bv_sample", (1, NS, 1, 2, HD))]


def t5_bucket(n):
    exact = 16
    nf = np.maximum(n, 1).astype(np.float32)
    large = exact + (np.log(nf / np.float32(exact)) / np.float32(math.log(2048 / exact))
                     * np.float32(16)).astype(np.int32)
    return np.where(n < exact, n, np.minimum(large, 31))


EXT = 3 * P
STEPS_OF = (1, 4, 16, 1)


def constants():
    hot = np.zeros((33, 4, EXT), np.float32)
    for kind, step in enumerate(STEPS_OF):
        for j in range(EXT):
            dist = 255 - j
            if 0 <= dist <= P:
                hot[t5_bucket(np.array(dist * step)), kind, j] = 8.0
            else:
                hot[32, kind, j] = 8.0 * NEG
    rows = np.arange(NS * NH)
    who = np.concatenate([rows[:, None] // NH == np.arange(NS), rows[:, None] % NH == np.arange(NH),
                          rows[:, None] % NH // 4 == np.arange(2)], 1).astype(np.float32)
    return {"const_hot": hot, "const_who": who}


def build(nc, io):
    ctx = ExitStack()
    with ctx:
        arena = Arena(nc)

        def sem(name):
            return ctx.enter_context(nc.semaphore(name))

        def dram(name, shape):
            return nc.dram_tensor(name, shape, F32, kind="Internal").ap()

        off = 0
        Y = arena.at("Y", [P, KT, T], F32, off); off += 4 * KT * T
        HOFF = off
        Hhi = arena.at("Hhi", [P, KT, T], F32R, off); off += 4 * KT * T
        Hlo = arena.at("Hlo", [P, KT, T], F32R, off); off += 4 * KT * T
        WOFF = off
        Whi, Wlo = [], []
        wbytes = 4 * KT * P

        def weight_slot(o):
            s = len(Whi)
            Whi.append(arena.at(f"Whi{s}", [P, KT, P], F32R, o))
            Wlo.append(arena.at(f"Wlo{s}", [P, KT, P], F32R, o + wbytes))
            return o + 2 * wbytes

        off = weight_slot(weight_slot(off))
        RAW = []
        for i in range(3):
            RAW.append(arena.at(f"RAW{i}", [P, KT, P], F32, off)); off += wbytes
        ident = arena.at("ident", [P, P], F32, off); off += 4 * P
        meanw = arena.at("meanw", [P, P], F32, off); off += 4 * P
        modT = arena.at("modT", [P, MT, NC1], F32, off); off += 4 * MT * NC1
        vecT = arena.at("vecT", [P, MT + 6 * KT], F32, off); off += 4 * (MT + 6 * KT)
        siluT = arena.at("siluT", [P, KT, 32], F32, off); off += 4 * KT * 32
        modrow = arena.at("modrow", [96, 2 * P], F32, off); off += 4 * 2 * P
        A9 = arena.at("A9", [P, KT, NC1], F32, off); off += 4 * KT * NC1
        B9 = arena.at("B9", [P, KT, NC1], F32, off); off += 4 * KT * NC1
        G9 = arena.at("G9", [P, KT, NC1], F32, off); off += 4 * KT * NC1
        yS = arena.at("yS", [P, KT, NS], F32, off); off += 4 * KT * NS
        yv = arena.at("yv", [P, 2, KT], F32, off); off += 4 * 2 * KT
        epst = arena.at("epst", [P, 8], F32, off); off += 32
        off = up32(off)
        BIG = off
        projT = arena.at("projT", [P, PT, T], F32, BIG)
        PROJ_END = BIG + up32(4 * PT * T)
        SIL, GF = [], []
        for i in range(2):
            SIL.append(arena.at(f"SIL{i}", [P, TG], F32, off)); off += up32(4 * TG)
        for i in range(2):
            GF.append(arena.at(f"GF{i}", [P, TG], F32, off)); off += up32(4 * TG)
        Ghi, Glo = [], []
        for j in range(2):
            Ghi.append(arena.at(f"Ghi{j}", [P, T], F32R, off)); off += 4 * T
            Glo.append(arena.at(f"Glo{j}", [P, T], F32R, off)); off += 4 * T
        for s in range(4):
            off = weight_slot(off)
        LNOFF = off
        ADA = []
        o = LNOFF
        for i in range(3):
            ADA.append(arena.at(f"ADA{i}", [P, KT, 2 * P], F32, o)); o += 4 * KT * 2 * P
        o = LNOFF
        SQ = arena.at("SQ", [P, KT, TG], F32, o); o += 4 * KT * TG
        HF = arena.at("HF", [P, KT, TG], F32, o); o += 4 * KT * TG
        SUM = arena.at("SUM", [P, TG], F32, o); o += up32(4 * TG)
        RSTD = arena.at("RSTD", [P, TG], F32, o); o += up32(4 * TG)
        XTOK = arena.at("XTOK", [P, TB, D], F32, HOFF)
        XSMP = arena.at("XSMP", [NS, D], F32, HOFF + 4 * TB * D)
        VROW = arena.at("VROW", [MT + 6 * KT, P], F32, HOFF + 4 * TB * D + 4 * D)
        CROW = arena.at("CROW", [NC1 * KT, P], F32, HOFF + 4 * TB * D + 4 * D + 4 * P)
        OUTT = [arena.at(f"OUTT{i}", [P, D], F32, HOFF + 4 * D * i) for i in range(4)]

        OUTS = arena.at("OUTS", [NS, D], F32, HOFF + 16 * D)

        psum = ctx.enter_context(nc.psum_tensor("psum", [P, 8, 512], F32))
        bank = [psum[:, i, :] for i in range(8)]
        MISC = 7

        def group(g):
            return slice(g * TG, (g + 1) * TG)

        def mm3(pe, out, whi, wlo, xhi, xlo, first, last):
            pe.matmul(out, whi, xhi, start=first, stop=False)
            pe.matmul(out, whi, xlo, start=False, stop=False)
            return pe.matmul(out, wlo, xhi, start=False, stop=last)

        rows_in, x_in, const_ready = sem("rows_in"), sem("x_in"), sem("const_ready")
        setup_pe, setup_act, setup_dve = sem("setup_pe"), sem("setup_act"), sem("setup_dve")
        ada_in = [sem(f"ada_in{i}") for i in range(3)]
        ada_done, ada_evac, ada_turned = sem("ada_done"), sem("ada_evac"), sem("ada_turned")
        mod_prep = sem("mod_prep")
        raw_in = [sem(f"raw_in{i}") for i in range(3)]
        out_stored = sem("out_stored")

        class Stream:

            def __init__(self, name):
                self.hi, self.ready = sem(name + "_w_hi"), sem(name + "_w_ready")

        class FFN:
            def __init__(self, n):
                self.n = n
                self.w = Stream(f"ffn{n}")
                self.up_done, self.down_done = sem(f"ffn{n}_up_done"), sem(f"ffn{n}_down_done")
                self.silu_done, self.gf_done = sem(f"ffn{n}_silu_done"), sem(f"ffn{n}_gf_done")
                self.g_hi, self.g_ready = sem(f"ffn{n}_g_hi"), sem(f"ffn{n}_g_ready")
                self.y_evac = sem(f"ffn{n}_y_evac")
                names = [f"ffn{n}_wg", f"ffn{n}_wu", f"ffn{n}_wd"]
                g, u, d = (io[x][0] for x in names)
                self.wg, self.wu = (x.rearrange("(k p) n -> p k n", p=P) for x in (g, u))
                self.wd = d

            def source(self, f, s):
                j = s // 2 if s < 4 else s - 4
                if s < 4:
                    return (self.wg, self.wu)[s % 2][:, :, bass.ds((f + j) * P, P)]
                return self.wd[bass.ds((f + j) * P, P), :].rearrange("p (k n) -> p k n", k=KT)

        ffn = {1: FFN(1), 2: FFN(2)}
        W = {"ffn1": ffn[1].w, "proj": Stream("proj"), "wout": Stream("wout"), "ffn2": ffn[2].w}
        PIECES = {"ffn1": 6 * CH, "proj": PT, "wout": KT, "ffn2": 6 * CH}
        RAW_BEFORE, count = {}, [0, 0, 0]
        for name in ("ffn1", "proj", "wout", "ffn2"):
            RAW_BEFORE[name] = list(count)
            ring = 3 if name.startswith("ffn") else 2
            for i in range(ring):
                count[i] += PIECES[name] // ring
        ORDER = ["ffn1", "proj", "wout", "ffn2"]

        proj_done, proj_evac = sem("proj_done"), sem("proj_evac")
        wout_done, wout_evac = sem("wout_done"), sem("wout_evac")

        class Norm:

            def __init__(self, name, norm, mod):
                self.norm, self.mod = norm, mod
                self.dve, self.act = sem(f"{name}_dve"), sem(f"{name}_act")
                self.pool, self.pe = sem(f"{name}_pool"), sem(f"{name}_pe")
                dve, act, pool, pe = [], [], [], []
                if norm and name != "init":
                    dve += ["prep"]
                for g in range(NG):
                    if norm:
                        dve += [(g, s) for s in ("sum", "center", "sumsq", "recip", "scale")]
                        act += [(g, "square"), (g, "std")]
                        pe += [(g, "mean"), (g, "var")]
                    if mod:
                        dve += [(g, "h")] + ([(g, "hs_mul"), (g, "hs_add")] if g == NG - 1 else [])
                        act += [(g, "hi")]
                        pool += [(g, "lo")]
                    dve += [(g, "y")]
                self.n_dve, self.n_act = Numbers(dve), Numbers(act)
                self.n_pool, self.n_pe = Numbers(pool), Numbers(pe)

        init = Norm("init", False, True)
        ln = {1: Norm("ln1", True, True), 2: Norm("ln2", True, True), 3: Norm("ln3", True, False)}
        H_READY = {"ffn1": init, "proj": ln[1], "ffn2": ln[2]}

        block = ctx.enter_context(nc.Block())

        def fetch(sp, phase, src, q, raw, use):
            sp.wait_ge(W[phase].ready, q + 1)
            sp.dma_start(RAW[raw][:, :, :], src).then_inc(raw_in[raw], 16)

        def split_hi(act, phase, slot, raw, use):
            act.wait_ge(raw_in[raw], use * 16 + 16 * (RAW_BEFORE[phase][raw] + 1))
            act.activation(Whi[slot][:, :, :], RAW[raw][:, :, :], ACT.Copy).then_inc(W[phase].hi, 1)

        def split_lo(pool, phase, slot, raw, q):
            pool.wait_ge(W[phase].hi, q + 1)
            pool.tensor_tensor(Wlo[slot][:, :, :], RAW[raw][:, :, :], Whi[slot][:, :, :].bitcast(F32),
                               ALU.subtract).then_inc(W[phase].ready, 1)

        def after_phase(sp, phase):
            i = ORDER.index(phase)
            if i:
                before = ORDER[i - 1]
                ring = 3 if before.startswith("ffn") else 2
                sp.wait_ge(W[before].ready, PIECES[before] + ring)

        def ffn_fetch_chunk(sp, x, c):
            for s in range(6):
                fetch(sp, f"ffn{x.n}", x.source(2 * c, s), 6 * c + s, s % 3, 2 * c + s // 3)

        def ffn_slot_free(eng, x, c, s):
            if s < 4:
                eng.wait_ge(x.up_done, 6 * c + 3 * (s // 2 + 1))
            else:
                eng.wait_ge(x.down_done, UNIT_D * c + UNIT_D)

        def ffn_split_hi(act, x, c, s):
            ffn_slot_free(act, x, c, s)
            split_hi(act, f"ffn{x.n}", s, s % 3, 2 * c + s // 3)

        def ffn_split_lo(pool, x, c, s):
            split_lo(pool, f"ffn{x.n}", s, s % 3, 6 * c + s)

        def ffn_pe(pe, x, c, ada=None):
            hready, hsem = H_READY[f"ffn{x.n}"], H_READY[f"ffn{x.n}"].pool
            for j in range(2):
                for g in range(NG):
                    u = 3 * j + g
                    gate, up = bank[2 * (u % 2)], bank[2 * (u % 2) + 1]
                    if g == 0:
                        pe.wait_ge(x.w.ready, 6 * c + 3 + 2 * (j + 1))
                    if j == 0:
                        pe.wait_ge(hsem, hready.n_pool[(g, "lo")])
                    pe.wait_ge(x.gf_done, 6 * c + u + 1)
                    for bk, s in ((gate, 2 * j), (up, 2 * j + 1)):
                        for k in range(KT):
                            last = mm3(pe, bk[:, 0:TG], Whi[s][:, k, :], Wlo[s][:, k, :],
                                       Hhi[:, k, group(g)], Hlo[:, k, group(g)], k == 0, k == KT - 1)
                    last.then_inc(x.up_done, 1)
            if ada is not None:
                ada_pe(pe, ada)
            pe.wait_ge(x.w.ready, 6 * c + 3 + 6)
            for g in range(NG):
                pe.wait_ge(x.g_ready, 6 * c + g + 6)
                for d in range(KT):
                    v = KT * g + d
                    bk = bank[4 + v % 3]
                    pe.wait_ge(x.y_evac, UNIT_D * c + v + 1)
                    for j in range(2):
                        last = mm3(pe, bk[:, 0:TG], Whi[4 + j][:, d, :], Wlo[4 + j][:, d, :],
                                   Ghi[j][:, group(g)], Glo[j][:, group(g)], j == 0, j == 1)
                    last.then_inc(x.down_done, 1)
                if ada is not None and g == 0:
                    ada_turn_pe(pe, ada)

        def ffn_act(act, x, c, more):
            for u in range(6):
                act.wait_ge(x.up_done, 6 * c + u + 7)
                act.wait_ge(x.gf_done, 6 * c + u + 1)
                act.activation(SIL[u % 2][:, :], bank[2 * (u % 2)][:, 0:TG], ACT.Silu).then_inc(x.silu_done, 1)
                act.wait_ge(x.down_done, UNIT_D * c + KT * (u % 3 + 1))
                act.wait_ge(x.gf_done, 6 * c + u + 3)
                act.activation(Ghi[u // 3][:, group(u % 3)], GF[u % 2][:, :], ACT.Copy).then_inc(x.g_hi, 1)
                if more and u == 2:
                    for s in (0, 1):
                        ffn_split_hi(act, x, c + 1, s)
            if more:
                for s in range(2, 6):
                    ffn_split_hi(act, x, c + 1, s)

        def ffn_dve(dve, x, c, ada=None):
            for u in range(6):
                dve.wait_ge(x.silu_done, 6 * c + u + 1)
                dve.wait_ge(x.g_ready, 6 * c + u + 1)
                dve.tensor_tensor(GF[u % 2][:, :], SIL[u % 2][:, :], bank[2 * (u % 2) + 1][:, 0:TG],
                                  ALU.mult).then_inc(x.gf_done, 1)
            if ada is not None:
                ada_dve(dve, ada)
            for g in range(NG):
                for d in range(KT):
                    v = KT * g + d
                    bk = bank[4 + v % 3]
                    n = TG if g < NG - 1 else PG
                    cols = slice(g * TG, g * TG + n)
                    dve.wait_ge(x.down_done, UNIT_D * c + v + UNIT_D + 1)
                    last = dve.scalar_tensor_tensor(Y[:, d, cols], bk[:, 0:n], G9[:, d, 0:1], Y[:, d, cols],
                                                    ALU.mult, ALU.add)
                    if g == NG - 1:
                        last = dve.tensor_tensor(yS[:, d, :], yS[:, d, :], bk[:, PG:TG], ALU.add)
                    last.then_inc(x.y_evac, 1)
                if ada is not None and g == 0:
                    ada_turn_dve(dve, ada)

        def ffn_pool(pool, x, c, more):
            for u in range(6):
                j, g = u // 3, u % 3
                pool.wait_ge(x.g_hi, 6 * c + u + 1)
                pool.tensor_tensor(Glo[j][:, group(g)], GF[u % 2][:, :], Ghi[j][:, group(g)].bitcast(F32),
                                   ALU.subtract).then_inc(x.g_ready, 1)
                if more and u == 2:
                    for s in (0, 1):
                        ffn_split_lo(pool, x, c + 1, s)
            if more:
                for s in range(2, 6):
                    ffn_split_lo(pool, x, c + 1, s)

        ADA_FIRST = 4
        ADA_ALL = MT // 6
        wada = io["w_ada"][0].rearrange("(k p) n -> p k n", p=P)

        def ada_fetch(sp, m):
            for i in range(3):
                sp.wait_ge(ada_done, m + 1)
                sp.dma_start(ADA[i][:, :, :], wada[:, :, bass.ds((6 * m + 2 * i) * P, 2 * P)]).then_inc(ada_in[i], 16)

        def ada_pe(pe, m):
            pe.wait_ge(ada_evac, 2 * m + 1)
            for i in range(3):
                pe.wait_ge(ada_in[i], 16 * m + 16)
                for k in range(KT):
                    last = pe.matmul(bank[MISC][32 * i:32 * i + 32, 0:2 * P], siluT[:, k, :], ADA[i][:, k, :],
                                     start=(k == 0), stop=(k == KT - 1))
            last.then_inc(ada_done, 1)

        def ada_turn_pe(pe, m):
            pe.wait_ge(ada_evac, 2 * m + 2)
            for j in range(2):
                last = pe.transpose(bank[MISC][:, 96 * j:96 * j + 96], modrow[:, j * P:(j + 1) * P],
                                    ident[0:96, 0:96])
            last.then_inc(ada_turned, 1)

        def ada_dve(dve, m):
            dve.wait_ge(ada_done, m + 2)
            dve.tensor_copy(modrow[:, :], bank[MISC][0:96, 0:2 * P]).then_inc(ada_evac, 1)

        def ada_turn_dve(dve, m):
            dve.wait_ge(ada_turned, m + 1)
            for j in range(2):
                bias = vecT[:, bass.ds(6 * m + j, 3, step=2)].unsqueeze(2).to_broadcast([P, 3, NC1])
                last = dve.tensor_tensor(modT[:, bass.ds(6 * m + j, 3, step=2), :],
                                         bank[MISC][:, 96 * j:96 * j + 96].rearrange("p (i n) -> p i n", n=32)[:, :, 0:NC1],
                                         bias, ALU.add)
            last.then_inc(ada_evac, 1)

        def mod(i):
            return modT[:, i * KT:(i + 1) * KT, :]

        def lnv(what, i):
            o = MT + (3 * KT if what == "b" else 0) + i * KT
            return vecT[:, o:o + KT]

        prep_steps = [0]

        def prep(dve, shift, scale, norm, last_norm=False):
            def step(ins):
                prep_steps[0] += 1
                ins.then_inc(mod_prep, 1)
                dve.wait_ge(mod_prep, prep_steps[0])

            if scale is not None:
                step(dve.tensor_scalar(A9[:, :, :], mod(scale), 1.0, None, ALU.add))
            if norm is None:
                step(dve.tensor_copy(B9[:, :, :], mod(shift)))
                step(dve.memset(yv[:, 0, :], ALPHA))
                step(dve.memset(yv[:, 1, :], 0.0))
                return
            g, b = lnv("g", norm), lnv("b", norm)
            if scale is not None:
                step(dve.tensor_tensor(B9[:, :, :], A9[:, :, :], b.unsqueeze(2).to_broadcast([P, KT, NC1]), ALU.mult))
                step(dve.tensor_tensor(B9[:, :, :], B9[:, :, :], mod(shift), ALU.add))
                step(dve.tensor_tensor(A9[:, :, :], A9[:, :, :], g.unsqueeze(2).to_broadcast([P, KT, NC1]), ALU.mult))
            a = 1.0 if last_norm else ALPHA
            step(dve.tensor_scalar(yv[:, 0, :], g, a, None, ALU.mult))
            step(dve.tensor_scalar(yv[:, 1, :], b, a, None, ALU.mult))

        def prep_gate(dve, which, factor):
            for ins in (lambda: dve.tensor_scalar(G9[:, :, :], mod(which), factor, None, ALU.mult),
                        lambda: dve.memset(yS[:, :, :], 0.0)):
                prep_steps[0] += 1
                ins().then_inc(mod_prep, 1)
                dve.wait_ge(mod_prep, prep_steps[0])

        def samples_in(dve):
            for ins in (lambda: dve.tensor_tensor(yS[:, :, :], yS[:, :, :], G9[:, :, 1:], ALU.mult),
                        lambda: dve.tensor_tensor(Y[:, :, TP:], Y[:, :, TP:], yS[:, :, :], ALU.add)):
                prep_steps[0] += 1
                ins().then_inc(mod_prep, 1)
                dve.wait_ge(mod_prep, prep_steps[0])

        def norm_dve(dve, n, g):
            def step(name, ins):
                ins.then_inc(n.dve, 1)
                dve.wait_ge(n.dve, n.n_dve[(g, name)])

            y = Y[:, :, group(g)]
            if n.norm:
                step("sum", dve.tensor_reduce(SUM[:, :], y.rearrange("p k t -> p t k"), AXX, ALU.add))
                dve.wait_ge(n.pe, n.n_pe[(g, "mean")])
                mean = bank[MISC][:, 0:TG].unsqueeze(1).to_broadcast([P, KT, TG])
                step("center", dve.tensor_tensor(y, y, mean, ALU.subtract))
                dve.wait_ge(n.act, n.n_act[(g, "square")])
                step("sumsq", dve.tensor_reduce(SUM[:, :], SQ[:, :, :].rearrange("p k t -> p t k"), AXX, ALU.add))
                dve.wait_ge(n.act, n.n_act[(g, "std")])
                step("recip", dve.reciprocal(RSTD[:, :], RSTD[:, :]))
                rstd = RSTD[:, :].unsqueeze(1).to_broadcast([P, KT, TG])
                step("scale", dve.tensor_tensor(y, y, rstd, ALU.mult))
            if n.mod:
                if g:
                    dve.wait_ge(n.pool, n.n_pool[(g - 1, "lo")])
                for k in range(KT):
                    last = dve.tensor_scalar(HF[:, k, :], Y[:, k, group(g)], A9[:, k, 0:1], B9[:, k, 0:1],
                                             ALU.mult, ALU.add)
                step("h", last)
                if g == NG - 1:
                    step("hs_mul", dve.tensor_tensor(HF[:, :, PG:], Y[:, :, TP:], A9[:, :, 1:], ALU.mult))
                    step("hs_add", dve.tensor_tensor(HF[:, :, PG:], HF[:, :, PG:], B9[:, :, 1:], ALU.add))
            for k in range(KT):
                last = dve.tensor_scalar(Y[:, k, group(g)], Y[:, k, group(g)], yv[:, 0, k:k + 1],
                                         yv[:, 1, k:k + 1], ALU.mult, ALU.add)
            step("y", last)

        def norm_act(act, n, g):
            if n.norm:
                act.wait_ge(n.dve, n.n_dve[(g, "center")])
                act.activation(SQ[:, :, :], Y[:, :, group(g)], ACT.Square).then_inc(n.act, 1)
                act.wait_ge(n.pe, n.n_pe[(g, "var")])
                act.activation(RSTD[:, :], bank[MISC][:, 0:TG], ACT.Sqrt, bias=epst[:, 0:1]).then_inc(n.act, 1)
            if n.mod:
                act.wait_ge(n.dve, n.n_dve[(g, "hs_add" if g == NG - 1 else "h")])
                act.activation(Hhi[:, :, group(g)], HF[:, :, :], ACT.Copy).then_inc(n.act, 1)

        def norm_pool(pool, n, g):
            pool.wait_ge(n.act, n.n_act[(g, "hi")])
            pool.tensor_tensor(Hlo[:, :, group(g)], HF[:, :, :], Hhi[:, :, group(g)].bitcast(F32),
                               ALU.subtract).then_inc(n.pool, 1)

        def norm_pe(pe, n, g):
            for name, src in (("mean", "sum"), ("var", "sumsq")):
                pe.wait_ge(n.dve, n.n_dve[(g, src)])
                pe.matmul(bank[MISC][:, 0:TG], meanw[:, :], SUM[:, :], start=True, stop=True).then_inc(n.pe, 1)

        win = io["w_in"][0].rearrange("(k p) n -> p k n", p=P)

        def pair_fetch(sp, phase, source, i):
            for j in range(2):
                fetch(sp, phase, source(2 * i + j), 2 * i + j, j, i)

        def pair_split_hi(act, phase, done, i, j):
            if done is not None:
                act.wait_ge(done, NG * (2 * i + j) - NG)
            split_hi(act, phase, j, j, i)

        def pair_pe(pe, phase, done, evac, i, h_numbers=None, h_sem=None):
            for j in range(2):
                pe.wait_ge(W[phase].ready, 2 * i + j + 3)
                for g in range(NG):
                    if h_sem is not None:
                        pe.wait_ge(h_sem, h_numbers[g])
                    u = NG * j + g
                    pe.wait_ge(evac, 6 * i + u + 1)
                    for k in range(KT):
                        last = mm3(pe, bank[u][:, 0:TG], Whi[j][:, k, :], Wlo[j][:, k, :],
                                   Hhi[:, k, group(g)], Hlo[:, k, group(g)], k == 0, k == KT - 1)
                    last.then_inc(done, 1)

        def proj_source(t):
            return win[:, :, bass.ds(t * P, P)]

        def proj_act(act, i, more):
            for j in range(2):
                for g in range(NG):
                    act.wait_ge(proj_done, 6 * i + NG * j + g + 1)
                    act.activation(projT[:, bass.ds(2 * i + j, 1), group(g)], bank[NG * j + g][:, 0:TG],
                                   ACT.Copy).then_inc(proj_evac, 1)
                if more:
                    pair_split_hi(act, "proj", proj_done, i + 1, j)

        wout = io["w_out"][0].rearrange("(k p) n -> p k n", p=P)

        def wout_source(t):
            return wout[:, :, bass.ds(t * P, P)]

        out_ready, out_pe, out_act = sem("out_ready"), sem("out_pe"), sem("out_act")
        out_slot = [sem(f"out_slot{i}") for i in range(4)]

        def dve_mark(dve, n):
            dve.nop().then_inc(n.dve, 1)

        def wout_dve(dve, i):
            for j in range(2):
                for g in range(NG):
                    n = TG if g < NG - 1 else PG
                    d, cols = 2 * i + j, slice(g * TG, g * TG + n)
                    bk = bank[NG * j + g]
                    dve.wait_ge(wout_done, 6 * i + NG * j + g + 1)
                    last = dve.scalar_tensor_tensor(Y[:, d, cols], bk[:, 0:n], G9[:, d, 0:1], Y[:, d, cols],
                                                    ALU.mult, ALU.add)
                    if g == NG - 1:
                        last = dve.tensor_tensor(yS[:, d, :], yS[:, d, :], bk[:, PG:TG], ALU.add)
                    last.then_inc(wout_evac, 1)

        SCALE = HD ** -0.5
        bias_rows = [dram(f"bias_rows{k}", (P, NH * EXT)) for k in range(4)]
        o = HOFF + 4 * TB * D + 4 * D + 8 * P
        BST = [arena.at(f"BST{i}", [P, NH, EXT], F32, o + 4 * NH * EXT * i) for i in range(2)]
        assert o + 8 * NH * EXT <= HOFF + 8 * KT * T
        HOT = arena.at("HOT", [33, 4, EXT], F32, BIG)
        REL = arena.at("REL", [33, 2 * NH], F32, BIG + 4 * 4 * EXT)
        RELX = arena.at("RELX", [33, 2 * NH, P], F32, BIG + 4 * 4 * EXT + 64)
        rel_in, rel_x, bias_mm, bias_ev, one_set = (sem(x) for x in ("rel_in", "rel_x", "bias_mm", "bias_ev", "one_set"))
        bias_st = [sem(f"bias_st{i}") for i in range(2)]

        AUG = HD + 1
        RW = NH * AUG + NH
        MAXO = NH * AUG
        o = HOFF
        VT = arena.at("VT", [P, TB, 10, AUG], F32, o); o += 4 * TB * 10 * AUG
        V4 = arena.at("V4", [P, TB, NH, AUG], F32, o); o += 4 * TB * NH * AUG
        V16 = arena.at("V16", [P, TB, NH, AUG], F32, o); o += 4 * TB * NH * AUG
        qS = []
        for i in range(2):
            qS.append(arena.at(f"qS{i}", [P, 4, P], F32, o)); o += 4 * 4 * P
        REC = []
        for i in range(2):
            REC.append(arena.at(f"REC{i}", [P, RW], F32, o)); o += up32(4 * RW)
        small = arena.at("small", [P, 8, 3 * NH], F32, o); o += 4 * 8 * 3 * NH
        parts = arena.at("parts", [P, 2], F32, o); o += 32
        sinkb = arena.at("sinkb", [P, NH], F32, o); o += 4 * NH
        assert o <= HOFF + 8 * KT * T, o - HOFF - 8 * KT * T
        SS = [arena.at(f"SS{i}", [P, 4, 2 * P], F32, WOFF + 4096 * i) for i in range(2)]
        PTB = [arena.at(f"PTB{i}", [P, 4, 2, P], F32, WOFF + 8192 + 4096 * i) for i in range(2)]
        o = BIG + 4 * T * TVA
        BIASB = arena.at("BIASB", [P, NH, 2 * P], F32, o)
        BIAS1 = arena.at("BIAS1", [P, NH, 2 * P], F32, o + 8192)
        MIX = arena.at("MIX", [P, D], F32, BIG + 4 * T * TVB)
        o = PROJ_END
        BIAS4 = arena.at("BIAS4", [P, NH, 2 * P], F32, o); o += 8192
        BIAS16 = arena.at("BIAS16", [P, NH, P], F32, o); o += 4096
        kB2 = arena.at("kB2", [P, TP], F32, o); o += 4096
        MR = arena.at("MR", [P, 3, RW], F32, WOFF + 16384)
        KST = [arena.at(f"KST{i}", [P, 10 * HD], F32, PROJ_END + 2560 * i) for i in range(4)]
        RS = arena.at("RS", [NS, PT * P], F32, WOFF)
        assert 3 * RW * 4 <= 3 * wbytes and 4 * NS * 0 + 4 * PT * P <= 16384

        scr16, scr4 = dram("scr16", (TP, RW)), dram("scr4", (TP, RW))
        q_rows = dram("q_rows", (NS, D))
        new_rows = dram("new_rows", (2, NS * NH))
        akp = io["ak_prompt"][0, 0].rearrange("t h d -> t (h d)")
        avp = io["av_prompt"][0, 0].rearrange("t h d -> t (h d)")
        av_heads = io["av_prompt"][0, 0]

        kv_turned, kv_evac, k_copied = sem("kv_turned"), sem("kv_evac"), sem("k_copied")
        k_stored = [sem(f"k_stored{i}") for i in range(4)]
        v_stored, b_in, v16_in, v4_in = sem("v_stored"), sem("b_in"), sem("v16_in"), sem("v4_in")
        q_staged, qk_done, max_done, sub_done, exp_done = (sem(x) for x in (
            "q_staged", "qk_done", "max_done", "sub_done", "exp_done"))
        t_done, t_evac, pv_done, o_evac = sem("t_done"), sem("t_evac"), sem("pv_done"), sem("o_evac")
        rec_stored = [sem(f"rec_stored{i}") for i in range(2)]
        branch_in, merge_step, merge_exp = sem("branch_in"), sem("merge_step"), sem("merge_exp")
        parts_set, max_begun = sem("parts_set"), sem("max_begun")
        mix_split_hi, mix_split, ones_set = sem("mix_split_hi"), sem("mix_split"), sem("ones_set")
        MIX_READY = [1, 2, 3]

        class Half:
            H = {"L": 2, "M": 4, "N": 4}
            COUNT = {"L": 8, "M": 4, "N": 8}
            BASE = {"L": 0, "M": 16, "N": 32}
            NEXT = {"L": "M", "M": "N"}
            BEFORE = {"M": "L", "N": "M"}

            def __init__(self, phase, i, l, even=None, half_i=None):
                self.phase, self.i, self.l = phase, i, l
                self.even = i % 2 == 0 if even is None else even
                self.half_i = i // 2 if half_i is None else half_i

            def step(self, n):
                h = self.H[self.phase]
                di, l = (self.l + n) // h, (self.l + n) % h
                i = self.i + di
                if isinstance(i, int) and i >= self.COUNT[self.phase]:
                    if self.phase == "N":
                        return None
                    return Half(self.NEXT[self.phase], 0, 0).step((i - self.COUNT[self.phase]) * h + l)
                if isinstance(i, int) and i < 0:
                    if self.phase == "L":
                        return None
                    b = self.BEFORE[self.phase]
                    return Half(b, self.COUNT[b] - 1, self.H[b] - 1).step(i * h + l + 1)
                if isinstance(i, int):
                    return Half(self.phase, i, l)
                even = self.even == (di % 2 == 0)
                half_i = self.half_i + (di // 2 if self.even else (di + 1) // 2)
                return Half(self.phase, i, l, even, half_i)

            @property
            def x(self):
                return self.BASE[self.phase] + self.H[self.phase] * self.i + self.l

            @property
            def y(self):
                if self.phase != "N" or (isinstance(self.i, int) and self.i == 0):
                    return self.x
                return 36 + 5 * (self.i - 1) + self.l + (self.l >= 2)

            @property
            def hh(self):
                return self.l % 2

            @property
            def parity(self):
                return self.l % 2

            @property
            def is_b(self):
                return self.phase == "N" and self.l < 2

            @property
            def blocks(self):
                if self.phase == "L":
                    return 1
                if self.phase == "M":
                    return 1 + self.l // 2
                return 1 if isinstance(self.i, int) and self.i == 0 else 2

            def columns(self, tile, keys):
                nb = self.blocks if keys else 1
                if self.phase == "L":
                    return tile.rearrange("p (j r) -> p r j", r=16)[:, bass.ds(2 * self.i, 2), :]
                if self.phase == "M":
                    b = self.l // 2
                    first = b + 1 - nb
                    return tile.rearrange("p (j r) -> p r j", r=4)[:, bass.ds(self.i, 1), first * P:(first + nb) * P]
                return tile[:, bass.ds((self.i + 1 - nb) * P, nb * P)]

            def bias(self, h):
                n = self.blocks * P
                if self.phase == "L":
                    return BIAS16[:, h, :]
                table = BIAS4 if self.phase == "M" else BIASB if self.is_b else BIAS1
                return table[:, h, 2 * P - n:2 * P]

            def values(self, h, kb):
                if self.phase == "L":
                    return V16[:, bass.ds(self.i, 1), h, :]
                if self.phase == "M":
                    return V4[:, bass.ds(2 * self.i + self.l // 2 + 1 - self.blocks + kb, 1), h, :]
                return VT[:, bass.ds(self.i + 1 - self.blocks + kb, 1), 8 + h // 4 if self.is_b else h, :]

            @property
            def record(self):
                if self.phase == "N" and not self.is_b:
                    return MR[:, 0, :]
                return REC[self.unit_parity][:, :]

            @property
            def unit_parity(self):
                if self.phase == "M":
                    return self.l // 2
                return 0 if self.even else 1

        def drive(eng, body, phase):
            n, h = Half.COUNT[phase], Half.H[phase]
            edge = 1 if phase == "M" else 2

            def block_of(i, even=None, half_i=None):
                for l in range(h):
                    body(Half(phase, i, l, even, half_i))

            for i in range(edge):
                block_of(i)
            if phase == "M":
                with eng.Fori(edge, n - edge) as i:
                    block_of(i, True, i)
            else:
                with eng.Fori(0, (n - 2 * edge) // 2) as ii:
                    block_of(2 * ii + edge, True, ii + 1)
                    block_of(2 * ii + edge + 1, False, ii + 1)
            for i in range(n - edge, n):
                block_of(i)

        def stage_q(pool, hf):
            if hf is None:
                return
            pool.wait_ge(qk_done, hf.x + 1)
            tile = (TQB if hf.is_b else TQA) + 2 * hf.hh
            mask = parts[:, :].unsqueeze(2).unsqueeze(3)
            for t in range(2):
                src = hf.columns(projT[:, tile + t, 0:TP], False)
                if hf.phase != "L":
                    src = src if hf.phase == "M" else src.rearrange("p (r j) -> p r j", r=1)
                r, n = src.shape[1:]
                last = pool.tensor_tensor(qS[hf.parity][:, 2 * t:2 * t + 2, :].rearrange("p o (r j) -> p o r j", r=r),
                                          src.unsqueeze(1).to_broadcast([P, 2, r, n]),
                                          mask.to_broadcast([P, 2, r, n]), ALU.mult)
            last.then_inc(q_staged, 1)

        def scores_pe(pe, hf):
            if hf is None:
                return
            pe.wait_ge(q_staged, hf.x + 1)
            pe.wait_ge(max_done, hf.x + 1)
            n = hf.blocks * P
            for j in range(4):
                h = 4 * hf.hh + j
                if hf.is_b:
                    keys = projT[:, TKB, 0:TP] if h % 2 == h // 4 else kB2[:, :]
                else:
                    keys = projT[:, TKA + h // 2, 0:TP]
                last = pe.matmul(bank[2 * hf.parity + j % 2][:, (j // 2) * 2 * P:(j // 2) * 2 * P + n],
                                 qS[hf.parity][:, j, :], hf.columns(keys, True),
                                 start=True, stop=True)
            last.then_inc(qk_done, 1)

        def max_dve(dve, hf):
            if hf is None:
                return
            dve.wait_ge(qk_done, hf.x + 3)
            if hf.step(-2) is not None:
                dve.wait_ge(t_done, hf.step(-2).y + 3)
            if hf.hh == 0:
                if hf.phase == "L":
                    if not (isinstance(hf.i, int) and hf.i < 2):
                        dve.wait_ge(rec_stored[hf.unit_parity], 32 * hf.half_i)
                elif hf.phase == "M":
                    dve.wait_ge(rec_stored[hf.unit_parity], 128 + 16 * hf.i)
                elif isinstance(hf.i, int) and hf.i < 2 and hf.is_b:
                    dve.wait_ge(rec_stored[hf.unit_parity], 192)
            n = hf.blocks * P
            dve.sem_inc(max_begun, 1)
            for j in range(4):
                h = 4 * hf.hh + j
                last = dve.tensor_tensor_reduce(
                    SS[hf.parity][:, j, 0:n],
                    bank[2 * hf.parity + j % 2][:, (j // 2) * 2 * P:(j // 2) * 2 * P + n], hf.bias(h),
                    SCALE, sinkb[:, h:h + 1] if hf.is_b else -3.0e38, ALU.add, ALU.max,
                    hf.record[:, MAXO + h:MAXO + h + 1])
            last.then_inc(max_done, 1)

        def sub_pool(pool, hf):
            if hf is None:
                return
            pool.wait_ge(max_done, hf.x + 3)
            n = hf.blocks * P
            s = SS[hf.parity][:, :, 0:n]
            m = hf.record[:, MAXO + 4 * hf.hh:MAXO + 4 * hf.hh + 4].unsqueeze(2).to_broadcast([P, 4, n])
            pool.tensor_tensor(s, s, m, ALU.subtract).then_inc(sub_done, 1)

        def exp_act(act, hf):
            if hf is None:
                return
            act.wait_ge(sub_done, hf.x + 1)
            s = SS[hf.parity][:, :, 0:hf.blocks * P]
            act.activation(s, s, ACT.Exp).then_inc(exp_done, 1)

        def turn_pe(pe, hf):
            pe.wait_ge(exp_done, hf.x + 1)
            pe.wait_ge(t_evac, hf.y + 1)
            for j in range(4):
                for kb in range(hf.blocks):
                    c = (j % 2) * 2 * P + kb * P
                    last = pe.transpose(bank[4 + j // 2][:, c:c + P], SS[hf.parity][:, j, kb * P:(kb + 1) * P],
                                        ident[:, :])
            last.then_inc(t_done, 1)

        def turn_act(act, hf):
            act.wait_ge(t_done, hf.y + 3)
            act.wait_ge(pv_done, hf.x + 1)
            nb = hf.blocks
            src = psum[:, 4:6, :].rearrange("p a (j k q) -> p (a j) k q", j=2, k=2)[:, :, 0:nb, :]
            act.activation(PTB[hf.parity][:, :, 0:nb, :], src, ACT.Copy).then_inc(t_evac, 1)

        def values_pe(pe, hf):
            if hf is None:
                return
            pe.wait_ge(t_evac, hf.y + 2)
            pe.wait_ge(o_evac, hf.x + 1)
            nb = hf.blocks
            for j in range(4):
                for kb in range(nb):
                    last = pe.matmul(bank[6 + hf.parity][:, j * AUG:(j + 1) * AUG], PTB[hf.parity][:, j, kb, :],
                                     hf.values(4 * hf.hh + j, kb), start=(kb == 0), stop=(kb == nb - 1))
            last.then_inc(pv_done, 1)

        def values_dve(dve, hf):
            if hf is None:
                return
            dve.wait_ge(pv_done, hf.x + 3)
            c = 4 * hf.hh * AUG
            dve.tensor_copy(hf.record[:, c:c + 4 * AUG], bank[6 + hf.parity][:, 0:4 * AUG]).then_inc(o_evac, 1)

        STEPS_B, STEPS_A = 4, 9

        def merge_at(b, what, n):
            return (STEPS_A + STEPS_B) * b + (STEPS_B if what == "a" else 0) + n

        def mix_y(b):
            return 71 if isinstance(b, int) and b == TB - 1 else 36 + 5 * b + 2

        def small_of(n, w):
            return small[:, n, 0:w]

        def merge_b_dve(dve, hf):
            b, rec = hf.i, hf.record
            recs = rec[:, 0:MAXO].rearrange("p (h a) -> p h a", a=AUG)
            n = [0]

            def step(ins):
                n[0] += 1
                ins.then_inc(merge_step, 1)
                dve.wait_ge(merge_step, merge_at(b, "b", n[0]))

            dve.wait_ge(o_evac, hf.x + 3)
            step(dve.tensor_tensor(small_of(0, NH), sinkb[:, :], rec[:, MAXO:MAXO + NH], ALU.subtract))
            dve.wait_ge(merge_exp, 2 * b + 1)
            step(dve.tensor_tensor(small_of(2, NH), small_of(1, NH), recs[:, :, HD], ALU.add))
            step(dve.reciprocal(small_of(3, NH), small_of(2, NH)))
            if not (isinstance(b, int) and b == 0):
                dve.wait_ge(t_done, mix_y(b - 1) + 3)
            step(dve.tensor_tensor(MIX[:, NH * HD:].rearrange("p (h a) -> p h a", a=HD), recs[:, :, 0:HD],
                                   small_of(3, NH).unsqueeze(2).to_broadcast([P, NH, HD]), ALU.mult))

        def merge_a_dve(dve, hf):
            b = hf.i
            outs = MR[:, :, 0:MAXO].rearrange("p s (h a) -> p s h a", a=AUG)
            maxima = MR[:, :, MAXO:MAXO + NH]
            n = [0]

            def step(ins):
                n[0] += 1
                ins.then_inc(merge_step, 1)
                dve.wait_ge(merge_step, merge_at(b, "a", n[0]))

            def three(i):
                return small[:, i, :].rearrange("p (s h) -> p s h", s=3)

            dve.wait_ge(o_evac, hf.x + 3)
            dve.wait_ge(branch_in, 32 * b + 32)
            step(dve.tensor_reduce(small_of(4, NH), maxima.rearrange("p s h -> p h s"), AXX, ALU.max))
            step(dve.tensor_tensor(three(5), maxima, small_of(4, NH).unsqueeze(1).to_broadcast([P, 3, NH]),
                                   ALU.subtract))
            dve.wait_ge(merge_exp, 2 * b + 2)
            step(dve.tensor_tensor(three(7), three(6), outs[:, :, :, HD], ALU.mult))
            step(dve.tensor_reduce(small_of(4, NH), three(7).rearrange("p s h -> p h s"), AXX, ALU.add))
            step(dve.reciprocal(small_of(4, NH), small_of(4, NH)))
            step(dve.tensor_tensor(three(7), three(6), small_of(4, NH).unsqueeze(1).to_broadcast([P, 3, NH]),
                                   ALU.mult))
            for s in range(3):
                last = dve.tensor_tensor(outs[:, s, :, 0:HD], outs[:, s, :, 0:HD],
                                         small[:, 7, s * NH:(s + 1) * NH].unsqueeze(2).to_broadcast([P, NH, HD]),
                                         ALU.mult)
            step(last)
            mix = MIX[:, 0:NH * HD].rearrange("p (h a) -> p h a", a=HD)
            step(dve.tensor_tensor(mix, outs[:, 0, :, 0:HD], outs[:, 1, :, 0:HD], ALU.add))
            step(dve.tensor_tensor(mix, mix, outs[:, 2, :, 0:HD], ALU.add))

        def merge_exp_act(act, hf):
            if hf.is_b:
                act.wait_ge(merge_step, merge_at(hf.i, "b", 1))
                act.activation(small_of(1, NH), small_of(0, NH), ACT.Exp).then_inc(merge_exp, 1)
            else:
                act.wait_ge(merge_step, merge_at(hf.i, "a", 2))
                act.activation(small_of(6, 3 * NH), small_of(5, 3 * NH), ACT.Exp).then_inc(merge_exp, 1)

        def mix_pe(pe, b):
            pe.wait_ge(merge_step, merge_at(b, "a", STEPS_A))
            pe.wait_ge(t_evac, mix_y(b) + 1)
            for t in range(KT):
                last = pe.transpose(bank[4 + t // 4][:, (t % 4) * P:(t % 4 + 1) * P], MIX[:, t * P:(t + 1) * P],
                                    ident[:, :])
            last.then_inc(t_done, 1)

        def mix_act(act, b):
            act.wait_ge(t_done, mix_y(b) + 3)
            for half, tile in enumerate((TQA, TQB)):
                last = act.activation(projT[:, tile:tile + 4, bass.ds(b * P, P)],
                                      bank[4 + half].rearrange("p (t q) -> p t q", q=P), ACT.Copy)
            last.then_inc(t_evac, 1)

        def mix_due(hf):
            return hf.phase == "N" and hf.l == 2 and not (isinstance(hf.i, int) and hf.i == 0)

        def merge_due(hf):
            return hf is not None and hf.phase == "N" and hf.l % 2 == 1

        def attn_pe(pe, hf):
            if mix_due(hf):
                mix_pe(pe, hf.i - 1)
            scores_pe(pe, hf.step(2))
            turn_pe(pe, hf)
            values_pe(pe, hf.step(-1))

        def attn_act(act, hf):
            if mix_due(hf):
                mix_act(act, hf.i - 1)
            turn_act(act, hf)
            if merge_due(hf.step(-1)):
                merge_exp_act(act, hf.step(-1))
            exp_act(act, hf.step(2))

        def attn_dve(dve, hf):
            before = hf.step(-1)
            values_dve(dve, before)
            if merge_due(before):
                (merge_b_dve if before.is_b else merge_a_dve)(dve, before)
            max_dve(dve, hf.step(2))

        def attn_pool(pool, hf):
            stage_q(pool, hf.step(3))
            sub_pool(pool, hf.step(2))

        LAST = Half("N", TB - 1, 3)

        def attn_sp(sp, hf):
            if hf.phase == "N":
                if hf.l == 0:
                    if not (isinstance(hf.i, int) and hf.i == 0):
                        sp.wait_ge(merge_step, merge_at(hf.i - 1, "a", STEPS_A))
                    for s, scr in ((1, scr4), (2, scr16)):
                        sp.dma_start(MR[:, s, :], scr[bass.ds(hf.i * P, P), :]).then_inc(branch_in, 16)
                return
            if hf.hh == 1:
                sp.wait_ge(o_evac, hf.x + 3)
                if hf.phase == "L":
                    rows = scr16.rearrange("(j r) c -> r j c", r=16)
                    for rr in range(2):
                        sp.dma_start(rows[bass.ds(2 * hf.i + rr, 1), :, :],
                                     REC[hf.unit_parity][HD * rr:HD * rr + HD, :]).then_inc(
                                         rec_stored[hf.unit_parity], 16)
                else:
                    rows = scr4.rearrange("(b p r) c -> r b p c", r=4, p=P)
                    sp.dma_start(rows[bass.ds(hf.i, 1), hf.l // 2, :, :], REC[hf.l // 2][:, :]).then_inc(
                        rec_stored[hf.l // 2], 16)

        def kv_pe(pe):
            for b in range(TB):
                if b:
                    pe.wait_ge(kv_evac, 2 * b)
                for which, tiles in enumerate((list(range(TKA, TKA + 4)) + [TKB], list(range(TVA, TVA + 4)) + [TVB])):
                    for n, t in enumerate(tiles):
                        last = pe.transpose(bank[2 * which + n // 4][:, (n % 4) * P:(n % 4 + 1) * P],
                                            projT[:, t, b * P:(b + 1) * P], ident[:, :])
                last.then_inc(kv_turned, 1)

        def kv_act(act):
            for b in range(TB):
                act.wait_ge(kv_turned, b + 1)
                if b >= 4:
                    act.wait_ge(k_stored[b % 4], 16)
                act.activation(KST[b % 4][:, 0:512], bank[0], ACT.Copy)
                act.activation(KST[b % 4][:, 512:640], bank[1][:, 0:P], ACT.Copy).then_inc(kv_evac, 1)

        def kv_dve(dve):
            for b in range(TB):
                dve.wait_ge(kv_evac, 2 * b + 1)
                dve.tensor_copy(VT[:, b, 0:NH, 0:HD], bank[2].rearrange("p (h a) -> p h a", a=HD))
                dve.tensor_copy(VT[:, b, NH:, 0:HD], bank[3][:, 0:P].rearrange("p (h a) -> p h a", a=HD)).then_inc(
                    kv_evac, 1)

        def kv_sp(sp):
            for b in range(TB):
                sp.wait_ge(kv_evac, 2 * b + 2)
                sp.dma_start(akp[b * P:(b + 1) * P, :], KST[b % 4][:, 0:512]).then_inc(k_stored[b % 4], 16)
                sp.dma_start(av_heads[b * P:(b + 1) * P, :, :], VT[:, b, 0:NH, 0:HD]).then_inc(v_stored, 16)
            sp.dma_start(io["bk_prompt"][0, 0].rearrange("t h d -> t (h d)"), KST[3][:, 512:640]).then_inc(out_stored, 16)
            sp.dma_start(io["bv_prompt"][0, 0], VT[:, TB - 1, NH:, 0:HD]).then_inc(out_stored, 16)

        def tables_sp(sp):
            sp.wait_ge(v_stored, 16 * TB)
            sp.wait_ge(samp_done, 1)
            v16 = av_heads.rearrange("(j r) h d -> r j h d", r=16)
            for u in range(TB):
                for rr in range(2):
                    sp.dma_start(V16[HD * rr:HD * rr + HD, u, :, 0:HD], v16[2 * u + rr]).then_inc(v16_in, 16)
            skew = [bass.AP(bias_rows[k].tensor, P - 1 + (P if k == 2 else 0),
                            [[NH * EXT - 1, P], [EXT, NH], [1, P if k == 2 else 2 * P]]) for k in range(4)]
            full = skew[2]
            rows = list(full.ap[0])
            sp.dma_start(BIAS16[0:HD, :, :], bass.AP(full.tensor, full.offset, [[rows[0], HD]] + [list(x) for x in full.ap[1:]])).then_inc(b_in, 16)
            sp.dma_start(BIAS16[HD:, :, HD:], bass.AP(full.tensor, full.offset + HD * rows[0] + HD,
                                                      [[rows[0], HD], [EXT, NH], [1, HD]])).then_inc(b_in, 16)
            sp.dma_start(BIAS4[:, :, :], skew[1]).then_inc(b_in, 16)
            sp.dma_start(BIAS1[:, :, :], skew[0]).then_inc(b_in, 16)
            sp.dma_start(BIASB[:, :, :], skew[3]).then_inc(b_in, 16)
            sp.dma_start(sinkb[:, :], bass.AP(io["sinks"].tensor, 0, [[0, P], [1, NH]])).then_inc(b_in, 16)
            v4 = av_heads.rearrange("(b p r) h d -> r b p h d", r=4, p=P)
            for r in range(4):
                for b in range(2):
                    sp.dma_start(V4[:, 2 * r + b, :, 0:HD], v4[r, b]).then_inc(v4_in, 16)
            for half in range(2):
                sp.dma_start(kB2[HD * half:HD * half + HD, :],
                             projT[HD * (1 - half):HD * (1 - half) + HD, TKB, 0:TP]).then_inc(b_in, 16)

        o = HOFF + 4 * TB * 10 * AUG
        KC = 3 * NH * HD + 2 * HD
        SK = [arena.at(f"SK{i}", [P, KC], F32, o + 4 * KC * i) for i in range(2)]
        o += 8 * KC
        QBC = [arena.at(f"QBC{i}", [P, D], F32, o + 4 * D * i) for i in range(2)]
        o += 8 * D
        PRD = arena.at("PRD", [P, 4, NH, HD], F32, o); o += 4 * 4 * NH * HD
        ROWS = NS * NH
        o = BIG + 4 * T * TVA
        sT = arena.at("sT", [P, 4, NS, NH], F32, o); o += 4 * 4 * ROWS
        SR = arena.at("SR", [ROWS, 4, P + 1], F32, o); o += up32(16 * (P + 1))
        SBIAS = arena.at("SBIAS", [ROWS, 4, P + 1], F32, o); o += up32(16 * (P + 1))
        SV1 = arena.at("SV1", [ROWS, 64], F32, o); o += 256
        NEW = arena.at("NEW", [NS, 2, NH, HD], F32, o); o += 4 * 2 * NH * HD
        SNEWT = arena.at("SNEWT", [NS, 2, NH], F32, o); o += 4 * 2 * NH
        o = PROJ_END
        PZ = arena.at("PZ", [P, NS, 4, ROWS], F32, o); o += 4 * NS * 4 * ROWS
        PN = arena.at("PN", [NS, 2, ROWS], F32, o); o += 8 * ROWS
        MA = arena.at("MA", [ROWS, NH, HD], F32, o); o += 4 * NH * HD
        MB = arena.at("MB", [ROWS, NH, HD], F32, o); o += 4 * NH * HD
        o = BIG + 4 * T * TVB
        OBG = arena.at("OBG", [ROWS, 2, HD], F32, o)
        OBS = arena.at("OBS", [ROWS, HD], F32, o + 512)
        DN = arena.at("DN", [ROWS, 2, NS], F32, o + 768)
        who = arena.at("who", [ROWS, NS + NH + 2], F32, o + 832)
        MAX_, NEGM, DEN, RDEN, PNEW, SNEW = (slice(2 * i, 2 * i + 2) for i in (0, 1, 2, 3, 4, 7))
        SINK, SINK8, ESINK = (slice(i, i + 1) for i in (11, 12, 13))
        samp_pe, samp_act, samp_dve = sem("samp_pe"), sem("samp_act"), sem("samp_dve")
        samp_done, q_out, new_out, new_in = (sem(x) for x in ("samp_done", "q_out", "new_out", "new_in"))
        samp_in = [sem(f"samp_in{i}") for i in range(2)]
        sampv_in = [sem(f"sampv_in{i}") for i in range(2)]
        samp_tables = sem("samp_tables")
        prd_done, red_done, sampv_done = sem("prd_done"), sem("red_done"), sem("sampv_done")

        def cache_rows(name, n, step):
            rows = io[name][0, n].rearrange("(p s) h d -> p s (h d)", s=step)
            return rows[rows.shape[0] - P:, 0, :]

        def samp_load(sp, what, n, slot, signal):
            for s, step in enumerate((1, 4, 16)):
                sp.dma_start(SK[slot][:, s * 512:(s + 1) * 512], cache_rows(f"cache_a_{what}", n, step)).then_inc(signal, 16)
            sp.dma_start(SK[slot][:, 1536:], cache_rows(f"cache_b_{what}", n, 1)).then_inc(signal, 16)

        def samp_sp(sp):
            sp.wait_ge(samp_dve, 1)
            sp.dma_start(q_rows[:, 0:512], RS[:, TQA * P:(TQA + 4) * P]).then_inc(q_out, 16)
            sp.dma_start(q_rows[:, 512:], RS[:, TQB * P:(TQB + 4) * P]).then_inc(q_out, 16)
            for name, t, w in (("ak_sample", TKA, 4), ("av_sample", TVA, 4), ("bk_sample", TKB, 1), ("bv_sample", TVB, 1)):
                sp.dma_start(io[name][0].rearrange("n t h d -> (n t) (h d)"), RS[:, t * P:(t + w) * P]).then_inc(out_stored, 16)
            sp.dma_start(who[:, :], io["const_who"]).then_inc(samp_tables, 16)
            sp.dma_start(SV1[:, SINK], bass.AP(io["sinks"].tensor, 0, [[0, NS], [1, NH], [1, 1]])).then_inc(samp_tables, 16)
            for k in range(4):
                sp.dma_start(SBIAS[:, k, :], bass.AP(bias_rows[k].tensor, P - 1, [[EXT, ROWS], [1, P + 1]])).then_inc(samp_tables, 16)
            sp.wait_ge(samp_dve, 3)
            sp.dma_start(new_rows.rearrange("a (n h) -> n a h", h=NH), SNEWT[:, :, :]).then_inc(new_out, 16)
            sp.wait_ge(q_out, 32)
            for n in range(NS):
                slot = n % 2
                if n >= 2:
                    sp.wait_ge(prd_done, n - 1)
                samp_load(sp, "k", n, slot, samp_in[slot])
                sp.dma_start(QBC[slot][:, :], bass.AP(q_rows.tensor, n * D, [[0, P], [1, D]])).then_inc(samp_in[slot], 16)
            sp.wait_ge(new_out, 16)
            for a in range(2):
                sp.dma_start(SV1[:, 14 + a:15 + a], bass.AP(new_rows.tensor, a * ROWS, [[1, ROWS], [1, 1]])).then_inc(new_in, 16)
            for n in range(NS):
                slot = n % 2
                if n < 2:
                    sp.wait_ge(prd_done, NS - 1 + slot)
                else:
                    sp.wait_ge(sampv_done, n - 1)
                samp_load(sp, "v", n, slot, sampv_in[slot])

        def samp_prod_pool(pool):
            for n in range(NS):
                slot = n % 2
                pool.wait_ge(samp_in[slot], 80 * (n // 2 + 1))
                if n:
                    pool.wait_ge(red_done, n)
                q = QBC[slot][:, 0:512].unsqueeze(1).to_broadcast([P, 3, 512])
                pool.tensor_tensor(PRD[:, 0:3, :, :].rearrange("p s h d -> p s (h d)"),
                                   SK[slot][:, 0:1536].rearrange("p (s c) -> p s c", s=3), q, ALU.mult)
                k = SK[slot][:, 1536:].rearrange("p (g d) -> p g d", g=2)
                for g in range(2):
                    last = pool.tensor_tensor(PRD[:, 3, 4 * g:4 * g + 4, :],
                                              QBC[slot][:, 512 + 256 * g:768 + 256 * g].rearrange("p (h d) -> p h d", h=4),
                                              k[:, g:g + 1, :].to_broadcast([P, 4, HD]), ALU.mult)
                last.then_inc(prd_done, 1)

        def samp_rows_pe(pe):
            for t in range(PT):
                last = pe.transpose(bank[t // 4][0:NS, (t % 4) * P:(t % 4 + 1) * P], projT[:, t, TP:], ident[:, :])
            last.then_inc(samp_pe, 1)

        def samp_pe_run(pe):
            pe.wait_ge(red_done, NS)
            for s in range(4):
                last = pe.transpose(bank[0][0:ROWS, s * P:(s + 1) * P], sT[:, s, :, :].rearrange("p n h -> p (n h)"), ident[:, :])
            last.then_inc(samp_pe, 1)
            pe.wait_ge(samp_dve, samp_at["d"])
            for s in range(4):
                pe.transpose(bank[1][:, s * ROWS:(s + 1) * ROWS], SR[:, s, 0:P], ident[0:ROWS, 0:ROWS])
            for a in range(2):
                last = pe.transpose(bank[2][0:NS, a * ROWS:(a + 1) * ROWS], DN[:, a, :], ident[0:ROWS, 0:ROWS])
            last.then_inc(samp_pe, 1)
            pe.wait_ge(samp_dve, samp_at["pz"])
            oa, ob = bank[3][0:ROWS, :], bank[4][0:ROWS, 0:2 * HD]
            for n in range(NS):
                slot = n % 2
                pe.wait_ge(sampv_in[slot], 64 * (n // 2 + 1))
                for s in range(3):
                    pe.matmul(oa, PZ[:, n, s, :], SK[slot][:, s * 512:(s + 1) * 512], start=(n == 0 and s == 0), stop=False)
                pe.matmul(ob, PZ[:, n, 3, :], SK[slot][:, 1536:], start=(n == 0), stop=False).then_inc(sampv_done, 1)
            pe.matmul(oa, PN[:, 0, :], RS[:, TVA * P:(TVA + 4) * P], start=False, stop=True)
            pe.matmul(ob, PN[:, 1, :], RS[:, TVB * P:(TVB + 1) * P], start=False, stop=True).then_inc(samp_pe, 1)
            pe.wait_ge(samp_dve, samp_at["mb"])
            for t in range(KT):
                src = (MA if t < 4 else MB)[:, 2 * (t % 4):2 * (t % 4) + 2, :].rearrange("p h d -> p (h d)")
                last = pe.matmul(bank[5][:, t * NS:(t + 1) * NS], src, who[:, 0:NS], start=True, stop=True)
            last.then_inc(samp_pe, 1)

        samp_at = Numbers(["rows", "new_mul", "new", "pz0", "bias", "newc", "max_a", "max_b", "sink8", "max_bs", "negm",
                           "den", "rden", "p_a", "p_b", "pnew_a", "pnew_b", "d_a", "d", "pz", "ma", "obg", "obs", "mb",
                           "out"])

        def samp_dve_run(dve):
            def step(name, ins):
                ins.then_inc(samp_dve, 1)
                dve.wait_ge(samp_dve, samp_at[name])

            dve.wait_ge(samp_pe, 1)
            for k in range(5):
                w = 512 if k < 4 else 256
                last = dve.tensor_copy(RS[:, k * 512:k * 512 + w], bank[k][0:NS, 0:w])
            step("rows", last)
            heads = RS[:, :].rearrange("p (h d) -> p h d", d=HD)
            dve.tensor_tensor(NEW[:, 0, :, :], heads[:, 0:8, :], heads[:, 8:16, :], ALU.mult)
            for g in range(2):
                last = dve.tensor_tensor(NEW[:, 1, 4 * g:4 * g + 4, :], heads[:, 24 + 4 * g:28 + 4 * g, :],
                                         heads[:, 32 + g:33 + g, :].to_broadcast([NS, 4, HD]), ALU.mult)
            step("new_mul", last)
            step("new", dve.tensor_reduce(SNEWT[:, :, :], NEW[:, :, :, :], AXX, ALU.add))
            for b in range(4):
                dve.wait_ge(k_stored[b], 32)
            dve.wait_ge(out_stored, 16 * 6)
            step("pz0", dve.memset(PZ[:, :, :, :], 0.0))
            for n in range(NS):
                dve.wait_ge(prd_done, n + 1)
                dve.tensor_reduce(sT[:, :, n, :], PRD[:, :, :, :], AXX, ALU.add).then_inc(red_done, 1)
            dve.wait_ge(samp_pe, 2)
            dve.wait_ge(samp_tables, 16 * 6)
            step("bias", dve.tensor_tensor(SR[:, :, 0:P], bank[0][0:ROWS, :].rearrange("p (s k) -> p s k", s=4),
                                           SBIAS[:, :, 0:P], ALU.add))
            dve.wait_ge(new_in, 32)
            dve.tensor_tensor(SR[:, 0:3, P:], SBIAS[:, 0:3, P:], SV1[:, 14:15].unsqueeze(1).to_broadcast([ROWS, 3, 1]), ALU.add)
            step("newc", dve.tensor_tensor(SR[:, 3, P:], SBIAS[:, 3, P:], SV1[:, 15:16], ALU.add))
            step("max_a", dve.tensor_reduce(SV1[:, 0:1], SR[:, 0:3, :].rearrange("p s k -> p (s k)"), AXX, ALU.max))
            step("max_b", dve.tensor_reduce(SV1[:, 1:2], SR[:, 3, :], AXX, ALU.max))
            step("sink8", dve.tensor_scalar(SV1[:, SINK8], SV1[:, SINK], 1.0 / SCALE, None, ALU.mult))
            step("max_bs", dve.tensor_tensor(SV1[:, 1:2], SV1[:, 1:2], SV1[:, SINK8], ALU.max))
            step("negm", dve.tensor_scalar(SV1[:, NEGM], SV1[:, MAX_], -SCALE, None, ALU.mult))
            dve.wait_ge(samp_act, 1)
            step("den", dve.tensor_tensor(SV1[:, 5:6], SV1[:, 5:6], SV1[:, ESINK], ALU.add))
            step("rden", dve.reciprocal(SV1[:, RDEN], SV1[:, DEN]))
            step("p_a", dve.tensor_scalar(SR[:, 0:3, :], SR[:, 0:3, :], SV1[:, 6:7], None, ALU.mult))
            step("p_b", dve.tensor_scalar(SR[:, 3, :], SR[:, 3, :], SV1[:, 7:8], None, ALU.mult))
            step("pnew_a", dve.tensor_reduce(SV1[:, 8:9], SR[:, 0:3, P], AXX, ALU.add))
            step("pnew_b", dve.tensor_copy(SV1[:, 9:10], SR[:, 3, P:]))
            step("d_a", dve.tensor_scalar(DN[:, 0, :], who[:, 0:NS], SV1[:, 8:9], None, ALU.mult))
            step("d", dve.tensor_scalar(DN[:, 1, :], who[:, 0:NS], SV1[:, 9:10], None, ALU.mult))
            dve.wait_ge(samp_pe, 3)
            pz = PZ[:, :, :, :]
            diag = bass.AP(pz.tensor, pz.offset, [list(pz.ap[0]), [4 * ROWS + NH, NS], [ROWS, 4], [1, NH]])
            dve.tensor_copy(diag, bank[1][:, 0:4 * ROWS].rearrange("p (s n h) -> p n s h", s=4, h=NH))
            step("pz", dve.tensor_copy(PN[:, :, :], bank[2][0:NS, 0:2 * ROWS].rearrange("p (a r) -> p a r", a=2)))
            dve.wait_ge(samp_pe, 4)
            own = who[:, NS:NS + NH].unsqueeze(2).to_broadcast([ROWS, NH, HD])
            step("ma", dve.tensor_tensor(MA[:, :, :], bank[3][0:ROWS, :].rearrange("p (h d) -> p h d", d=HD), own, ALU.mult))
            step("obg", dve.tensor_tensor(OBG[:, :, :], bank[4][0:ROWS, 0:2 * HD].rearrange("p (g d) -> p g d", g=2),
                                          who[:, NS + NH:].unsqueeze(2).to_broadcast([ROWS, 2, HD]), ALU.mult))
            step("obs", dve.tensor_tensor(OBS[:, :], OBG[:, 0, :], OBG[:, 1, :], ALU.add))
            step("mb", dve.tensor_tensor(MB[:, :, :], OBS[:, :].unsqueeze(1).to_broadcast([ROWS, NH, HD]), own, ALU.mult))
            dve.wait_ge(samp_pe, 5)
            o5 = bank[5][:, 0:KT * NS].rearrange("p (t n) -> p t n", n=NS)
            dve.tensor_copy(projT[:, TQA:TQA + 4, TP:], o5[:, 0:4, :])
            step("out", dve.tensor_copy(projT[:, TQB:TQB + 4, TP:], o5[:, 4:8, :]))
            dve.sem_inc(samp_done, 1)

        def samp_act_run(act):
            act.wait_ge(samp_dve, samp_at["negm"])
            flat = SR[:, 0:3, :].rearrange("p s k -> p (s k)")
            act.activation(flat, flat, ACT.Exp, bias=SV1[:, 2:3], scale=SCALE, accum_out=SV1[:, 4:5])
            act.activation(SR[:, 3, :], SR[:, 3, :], ACT.Exp, bias=SV1[:, 3:4], scale=SCALE, accum_out=SV1[:, 5:6])
            act.activation(SV1[:, ESINK], SV1[:, SINK], ACT.Exp, bias=SV1[:, 3:4]).then_inc(samp_act, 1)


        def out_half(eng, b, half):
            rows = P if b < TB else NS
            dst = OUTT[b % 4] if b < TB else OUTS
            eng.wait_ge(out_pe, b + 1)
            if 4 <= b < TB:
                eng.wait_ge(out_slot[b % 4], 16 * (b // 4))
            src = bank[2 * (b % 2) + half][0:rows, :]
            out = dst[0:rows, half * 512:(half + 1) * 512]
            if half:
                eng.activation(out, src, ACT.Copy).then_inc(out_act, 1)
            else:
                eng.wait_ge(out_act, b + 1)
                eng.tensor_copy(out, src).then_inc(out_ready, 1)

        @block.sync
        def _(sp):
            VA = VROW
            sp.dma_start(CROW[0:KT, :], io["c_prompt"].rearrange("n (k p) -> (n k) p", p=P)).then_inc(rows_in, 16)
            sp.dma_start(CROW[KT:, :], io["c_sample"].rearrange("n (k p) -> (n k) p", p=P)).then_inc(rows_in, 16)
            sp.dma_start(VA[0:MT, :], io["b_ada"].rearrange("l (k p) -> (l k) p", p=P)).then_inc(rows_in, 16)
            sp.dma_start(VA[MT:MT + 3 * KT, :], io["ln_g"].rearrange("l i (k p) -> (l i k) p", p=P)).then_inc(rows_in, 16)
            sp.dma_start(VA[MT + 3 * KT:, :], io["ln_b"].rearrange("l i (k p) -> (l i k) p", p=P)).then_inc(rows_in, 16)
            ada_fetch(sp, 0)
            sp.dma_start(XTOK[:, :, :], io["x_prompt"][0].rearrange("(b p) d -> p b d", p=P)).then_inc(x_in, 16)
            sp.dma_start(XSMP[:, :], io["x_sample"].rearrange("n t d -> (n t) d")).then_inc(x_in, 16)
            sp.dma_start(HOT[:, :, :], io["const_hot"]).then_inc(rel_in, 16)
            sp.wait_ge(one_set, 1)
            sp.dma_start(REL[0:32, :], io["rel_bias"]).then_inc(rel_in, 16)
            for k in range(4):
                sp.wait_ge(bias_ev, NH * (k + 1))
                sp.dma_start(bias_rows[k], BST[k % 2][:, :, :].rearrange("p h e -> p (h e)")).then_inc(bias_st[k % 2], 16)
            with sp.Fori(1, ADA_FIRST) as m:
                ada_fetch(sp, m)
            ffn_fetch_chunk(sp, ffn[1], 0)
            sp.wait_ge(init.pool, init.n_pool[(NG - 1, "lo")])
            ada_fetch(sp, ADA_FIRST)
            with sp.Fori(0, ADA_ALL - ADA_FIRST - 1) as c:
                ffn_fetch_chunk(sp, ffn[1], c + 1)
                ada_fetch(sp, c + ADA_FIRST + 1)
            with sp.Fori(ADA_ALL - ADA_FIRST - 1, CH - 1) as c:
                ffn_fetch_chunk(sp, ffn[1], c + 1)
            after_phase(sp, "proj")
            with sp.Fori(0, PT // 2) as i:
                pair_fetch(sp, "proj", proj_source, i)
            kv_sp(sp)
            samp_sp(sp)
            tables_sp(sp)
            for phase in "LMN":
                if phase == "N":
                    for i in range(2):
                        sp.wait_ge(rec_stored[i], 192)
                drive(sp, lambda hf: attn_sp(sp, hf), phase)
            sp.wait_ge(merge_step, merge_at(TB - 1, "a", STEPS_A))
            after_phase(sp, "wout")
            with sp.Fori(0, KT // 2) as i:
                pair_fetch(sp, "wout", wout_source, i)
            after_phase(sp, "ffn2")
            with sp.Fori(0, CH) as c:
                ffn_fetch_chunk(sp, ffn[2], c)
            for b in range(TB):
                sp.wait_ge(out_ready, b + 1)
                sp.dma_start(io["y_prompt"][0, b * P:(b + 1) * P, :], OUTT[b % 4][:, :]).then_inc(out_slot[b % 4], 16)
            sp.wait_ge(out_ready, TB + 1)
            sp.dma_start(io["y_sample"].rearrange("n t d -> (n t) d"), OUTS[:, :]).then_inc(out_stored, 16)
            sp.wait_ge(out_stored, 16 * 7)
            for i in range(4):
                sp.wait_ge(out_slot[i], 16 * (TB // 4))

        @block.gpsimd
        def _(pool):
            pool.memset(ident[:, :], 0.0).then_inc(const_ready, 1)
            pool.wait_ge(const_ready, 1)
            pool.affine_select(out=ident[:, :], in_=ident[:, :], compare_op=ALU.not_equal, fill=1.0, base=0,
                               pattern=[[-1, P]], channel_multiplier=1).then_inc(const_ready, 1)
            pool.memset(meanw[:, :], 1.0 / D).then_inc(const_ready, 1)
            pool.memset(epst[:, :], EPS).then_inc(const_ready, 1)
            for name in ORDER:
                pool.sem_inc(W[name].ready, 3 if name.startswith("ffn") else 2)
            for n in (1, 2):
                pool.sem_inc(ffn[n].g_ready, 2)
            pool.memset(REL[:, :], 1.0).then_inc(one_set, 1)
            pool.sem_inc(t_evac, 1)
            for s in range(6):
                ffn_split_lo(pool, ffn[1], 0, s)
            for g in range(NG):
                norm_pool(pool, init, g)
            with pool.Fori(0, CH - 1) as c:
                ffn_pool(pool, ffn[1], c, True)
            ffn_pool(pool, ffn[1], CH - 1, False)
            for j in range(2):
                split_lo(pool, "proj", j, j, j)
            for g in range(NG):
                norm_pool(pool, ln[1], g)
            with pool.Fori(1, PT // 2) as i:
                for j in range(2):
                    split_lo(pool, "proj", j, j, 2 * i + j)
            pool.wait_ge(kv_evac, 2 * TB)
            samp_prod_pool(pool)
            pool.memset(VT[:, :, :, HD:], 1.0)
            pool.wait_ge(samp_done, 1)
            pool.memset(V16[:, :, :, HD:], 1.0)
            pool.memset(V4[:, :, :, HD:], 1.0).then_inc(ones_set, 1)
            pool.wait_ge(parts_set, 1)
            for x in range(3):
                stage_q(pool, Half("L", 0, 0).step(x))
            for x in range(2):
                sub_pool(pool, Half("L", 0, 0).step(x))
            for phase in "LMN":
                drive(pool, lambda hf: attn_pool(pool, hf), phase)
            for g in range(NG):
                pool.wait_ge(mix_split_hi, g + 1)
                for half, tile in enumerate((TQA, TQB)):
                    last = pool.tensor_tensor(Hlo[:, 4 * half:4 * half + 4, group(g)], projT[:, tile:tile + 4, group(g)],
                                              Hhi[:, 4 * half:4 * half + 4, group(g)].bitcast(F32), ALU.subtract)
                last.then_inc(mix_split, 1)
            with pool.Fori(0, KT // 2) as i:
                for j in range(2):
                    split_lo(pool, "wout", j, j, 2 * i + j)
            for s in range(6):
                ffn_split_lo(pool, ffn[2], 0, s)
            for g in range(NG):
                norm_pool(pool, ln[2], g)
            with pool.Fori(0, CH - 1) as c:
                ffn_pool(pool, ffn[2], c, True)
            ffn_pool(pool, ffn[2], CH - 1, False)

        XU = TB // 4 * KT

        @block.scalar
        def _(act):
            act.wait_ge(setup_pe, 2)
            act.wait_ge(setup_dve, 1)
            act.activation(siluT[:, :, 0:NC1].rearrange("p k n -> p n k"),
                           bank[1][:, 0:NC1 * KT].rearrange("p (n k) -> p n k", k=KT), ACT.Silu).then_inc(setup_act, 1)
            for u in range(XU):
                act.wait_ge(setup_pe, 3 + u)
                k, h = u // 2, u % 2
                act.activation(Y[:, k, h * 512:(h + 1) * 512], bank[2 + u % 4][:, :], ACT.Copy).then_inc(setup_act, 1)
            act.wait_ge(setup_pe, 3 + XU)
            act.activation(Y[:, :, TP:], bank[6][:, 0:KT * NS].rearrange("p (k n) -> p k n", n=NS),
                           ACT.Copy).then_inc(setup_act, 1)
            for s in range(6):
                split_hi(act, "ffn1", s, s % 3, s // 3)
            for g in range(NG):
                norm_act(act, init, g)
            with act.Fori(0, CH - 1) as c:
                ffn_act(act, ffn[1], c, True)
            ffn_act(act, ffn[1], CH - 1, False)
            act.wait_ge(ffn[1].up_done, 6 * CH + 6)
            for j in range(2):
                pair_split_hi(act, "proj", None, 0, j)
            for g in range(NG):
                norm_act(act, ln[1], g)
            with act.Fori(0, PT // 2 - 1) as i:
                proj_act(act, i, True)
            proj_act(act, PT // 2 - 1, False)
            kv_act(act)
            samp_act_run(act)
            for x in range(2):
                exp_act(act, Half("L", 0, 0).step(x))
            for phase in "LMN":
                drive(act, lambda hf: attn_act(act, hf), phase)
            merge_exp_act(act, LAST)
            mix_act(act, TB - 1)
            act.wait_ge(t_evac, 73)
            for g in range(NG):
                for half, tile in enumerate((TQA, TQB)):
                    last = act.activation(Hhi[:, 4 * half:4 * half + 4, group(g)], projT[:, tile:tile + 4, group(g)],
                                          ACT.Copy)
                last.then_inc(mix_split_hi, 1)
            for j in range(2):
                pair_split_hi(act, "wout", None, 0, j)
            with act.Fori(1, KT // 2) as i:
                for j in range(2):
                    pair_split_hi(act, "wout", wout_done, i, j)
            act.wait_ge(wout_done, NG * KT)
            for s in range(6):
                split_hi(act, "ffn2", s, s % 3, s // 3)
            for g in range(NG):
                norm_act(act, ln[2], g)
            with act.Fori(0, CH - 1) as c:
                ffn_act(act, ffn[2], c, True)
            ffn_act(act, ffn[2], CH - 1, False)
            for g in range(NG):
                norm_act(act, ln[3], g)
            for b in range(TB + 1):
                out_half(act, b, 1)

        @block.vector
        def _(dve):
            for n in (1, 2):
                dve.sem_inc(ffn[n].gf_done, 2)
                dve.sem_inc(ffn[n].y_evac, 3)
            dve.sem_inc(ada_evac, 1)
            for s in (max_done, o_evac):
                dve.sem_inc(s, 2)
            dve.sem_inc(proj_evac, 6)
            dve.sem_inc(wout_evac, 6)
            dve.memset(siluT[:, :, :], 0.0).then_inc(setup_dve, 1)
            dve.wait_ge(setup_pe, 1)
            dve.tensor_copy(vecT[:, :], bank[0][:, 0:MT + 6 * KT]).then_inc(setup_dve, 1)
            dve.wait_ge(setup_dve, 2)
            dve.wait_ge(rel_in, 32)
            dve.tensor_copy(RELX[:, :, :], REL[:, :].unsqueeze(2).to_broadcast([33, 2 * NH, P])).then_inc(rel_x, 1)
            for n in range(4 * NH):
                k, h = n // NH, n % NH
                if k >= 2 and h == 0:
                    dve.wait_ge(bias_st[k % 2], 16)
                dve.wait_ge(bias_mm, n + 1)
                dve.tensor_copy(BST[k % 2][:, h, :], bank[n % 2][:, 0:EXT]).then_inc(bias_ev, 1)
            for k in range(2):
                dve.wait_ge(bias_st[k], 32)
            with dve.Fori(0, ADA_FIRST) as m:
                ada_dve(dve, m)
                ada_turn_dve(dve, m)
            dve.wait_ge(ada_evac, 2 * ADA_FIRST + 1)
            prep(dve, 0, 1, None)
            prep_gate(dve, 2, 0.5)
            dve.wait_ge(setup_act, 2 + XU)
            for g in range(NG):
                norm_dve(dve, init, g)
            with dve.Fori(0, ADA_ALL - ADA_FIRST) as c:
                ffn_dve(dve, ffn[1], c, c + ADA_FIRST)
            with dve.Fori(ADA_ALL - ADA_FIRST, CH) as c:
                ffn_dve(dve, ffn[1], c)
            dve.wait_ge(ada_evac, 2 * ADA_ALL + 1)
            dve.wait_ge(ffn[1].y_evac, UNIT_D * CH + 3)
            samples_in(dve)
            prep(dve, 3, 4, 0)
            prep_gate(dve, 5, 1.0)
            dve_mark(dve, ln[1])
            for g in range(NG):
                norm_dve(dve, ln[1], g)
            kv_dve(dve)
            samp_dve_run(dve)
            dve.memset(BIAS16[HD:, :, 0:HD], NEG / SCALE)
            dve.memset(parts[0:HD, 0:1], 1.0)
            dve.memset(parts[0:HD, 1:2], 0.0)
            dve.memset(parts[HD:, 0:1], 0.0)
            dve.memset(parts[HD:, 1:2], 1.0).then_inc(parts_set, 1)
            dve.wait_ge(parts_set, 1)
            dve.wait_ge(b_in, 16 * 8)
            for x in range(2):
                max_dve(dve, Half("L", 0, 0).step(x))
            for phase in "LMN":
                drive(dve, lambda hf: attn_dve(dve, hf), phase)
            values_dve(dve, LAST)
            merge_a_dve(dve, LAST)
            with dve.Fori(0, KT // 2) as i:
                wout_dve(dve, i)
            dve.wait_ge(wout_evac, NG * KT + 6)
            samples_in(dve)
            prep(dve, 6, 7, 1)
            prep_gate(dve, 8, 0.5)
            dve_mark(dve, ln[2])
            for g in range(NG):
                norm_dve(dve, ln[2], g)
            with dve.Fori(0, CH) as c:
                ffn_dve(dve, ffn[2], c)
            dve.wait_ge(ffn[2].y_evac, UNIT_D * CH + 3)
            samples_in(dve)
            prep(dve, None, None, 2, last_norm=True)
            dve_mark(dve, ln[3])
            for g in range(NG):
                norm_dve(dve, ln[3], g)
            for b in range(TB + 1):
                out_half(dve, b, 0)

        @block.tensor
        def _(pe):
            for n in (1, 2):
                pe.sem_inc(ffn[n].up_done, 6)
                pe.sem_inc(ffn[n].down_done, UNIT_D)
            for s in (qk_done, t_done, pv_done):
                pe.sem_inc(s, 2)
            pe.sem_inc(ada_done, 1)
            pe.wait_ge(const_ready, 4)
            pe.wait_ge(rows_in, 80)
            nv = MT + 6 * KT
            pe.transpose(bank[0][:, 0:nv], VROW[:, :], ident[0:nv, 0:nv]).then_inc(setup_pe, 1)
            nc_ = NC1 * KT
            pe.transpose(bank[1][:, 0:nc_], CROW[:, :], ident[0:nc_, 0:nc_]).then_inc(setup_pe, 1)
            pe.wait_ge(x_in, 32)
            for u in range(XU):
                k, h = u // 2, u % 2
                if u >= 4:
                    pe.wait_ge(setup_act, 1 + u - 3)
                for b in range(4):
                    last = pe.transpose(bank[2 + u % 4][:, b * P:(b + 1) * P],
                                        XTOK[:, 4 * h + b, k * P:(k + 1) * P], ident[:, :])
                last.then_inc(setup_pe, 1)
            for k in range(KT):
                last = pe.transpose(bank[6][:, k * NS:(k + 1) * NS], XSMP[:, k * P:(k + 1) * P],
                                    ident[0:NS, 0:NS])
            last.then_inc(setup_pe, 1)
            pe.wait_ge(rel_x, 1)
            pe.wait_ge(setup_act, 1)
            for n in range(4 * NH):
                k, h = n // NH, n % NH
                if n >= 2:
                    pe.wait_ge(bias_ev, n - 1)
                pe.matmul(bank[n % 2][:, 0:EXT], RELX[:, h + (NH if k == 3 else 0), :], HOT[:, k, :],
                          start=True, stop=True).then_inc(bias_mm, 1)
            pe.wait_ge(setup_act, 1)
            with pe.Fori(0, ADA_FIRST) as m:
                ada_pe(pe, m)
                ada_turn_pe(pe, m)
            with pe.Fori(0, ADA_ALL - ADA_FIRST) as c:
                ffn_pe(pe, ffn[1], c, c + ADA_FIRST)
            with pe.Fori(ADA_ALL - ADA_FIRST, CH) as c:
                ffn_pe(pe, ffn[1], c)
            for g in range(NG):
                norm_pe(pe, ln[1], g)
            lo = [ln[1].n_pool[(g, "lo")] for g in range(NG)]
            with pe.Fori(0, PT // 2) as i:
                pair_pe(pe, "proj", proj_done, proj_evac, i, lo, ln[1].pool)
            pe.wait_ge(proj_evac, NG * PT + 6)
            kv_pe(pe)
            pe.wait_ge(kv_evac, 2 * TB)
            samp_rows_pe(pe)
            samp_pe_run(pe)
            pe.wait_ge(samp_done, 1)
            pe.wait_ge(b_in, 16 * 8)
            for x in range(2):
                scores_pe(pe, Half("L", 0, 0).step(x))
            pe.wait_ge(ones_set, 1)
            pe.wait_ge(v16_in, 16 * 2 * TB)
            pe.wait_ge(v4_in, 16 * TB)
            for phase in "LMN":
                drive(pe, lambda hf: attn_pe(pe, hf), phase)
            values_pe(pe, LAST)
            mix_pe(pe, TB - 1)
            with pe.Fori(0, KT // 2) as i:
                pair_pe(pe, "wout", wout_done, wout_evac, i, MIX_READY, mix_split)
            for g in range(NG):
                norm_pe(pe, ln[2], g)
            with pe.Fori(0, CH) as c:
                ffn_pe(pe, ffn[2], c)
            for g in range(NG):
                norm_pe(pe, ln[3], g)
            pe.wait_ge(ln[3].dve, ln[3].n_dve[(NG - 1, "y")])
            for b in range(TB + 1):
                cols = slice(b * P, (b + 1) * P) if b < TB else slice(TP, T)
                rows = P if b < TB else NS
                if b >= 2:
                    pe.wait_ge(out_ready, b - 1)
                for k in range(KT):
                    last = pe.transpose(bank[2 * (b % 2) + k // 4][0:rows, (k % 4) * P:(k % 4 + 1) * P],
                                        Y[:, k, cols], ident[:, :])
                last.then_inc(out_pe, 1)


def kernel(**inputs):
    import numpy as _np
    import concourse.bacc as _bacc
    from concourse import mybir as _mybir
    from concourse.bass_utils import run_bass_kernel_spmd as _run

    nc = _bacc.Bacc("TRN2", target_bir_lowering=False, num_devices=1, dynamic_dma_scratch_size=1024)
    arrays, io = {}, {}
    for name, a in list(inputs.items()) + list(constants().items()):
        a = _np.ascontiguousarray(a)
        arrays[f"in_{name}"] = a
        io[name] = nc.dram_tensor(f"in_{name}", a.shape, _mybir.dt.from_np(a.dtype), kind="ExternalInput").ap()
    for name, shape in OUTPUTS:
        io[name] = nc.dram_tensor(f"out_{name}", shape, _mybir.dt.float32, kind="ExternalOutput").ap()
    build(nc, io)
    r = _run(nc, [arrays], core_ids=[0])
    return tuple(r.results[0][f"out_{name}"] for name, _ in OUTPUTS)
```

```python
import math
from contextlib import ExitStack

import numpy as np

import concourse.bass as bass
from concourse import mybir

P = 128
D = 1024
KT = D // P
TP = 1024
NS = 8
T = TP + NS
TB = TP // P
NG = 3
TG = T // NG
PG = TG - NS
FF = 2816
FT = FF // P
CH = FT // 2
HD = 64
NH = 8
PT = 18
TQA, TKA, TVA, TQB, TKB, TVB = 0, 4, 8, 12, 16, 17
MODS = 9
MT = MODS * KT
NC1 = 1 + NS
ALPHA = 2.0 ** 0.25
EPS = 1e-5
NEG = -1e30
UNIT_D = NG * KT

F32 = mybir.dt.float32
F32R = mybir.dt.float32r
ALU = mybir.AluOpType
ACT = mybir.ActivationFunctionType
AXX = mybir.AxisListType.X


class Arena:

    def __init__(self, nc):
        self.nc, self.base = nc, (nc.sbuf_base + 31) // 32 * 32

    def at(self, name, shape, dtype, offset):
        size = 4 * int(np.prod(shape[1:]))
        assert offset % 32 == 0 and self.base + offset + size <= self.nc.sbuf_usable_end, (name, offset, size)
        return self.nc.alloc_sbuf_tensor_at(name, shape, dtype, offset=self.base + offset)


def up32(n):
    return (n + 31) // 32 * 32


class Numbers:

    def __init__(self, steps):
        self.of = {s: n + 1 for n, s in enumerate(steps)}
        self.total = len(self.of)

    def __getitem__(self, step):
        return self.of[step]

OUTPUTS = [("y_prompt", (1, TP, D)), ("y_sample", (NS, 1, D)),
           ("ak_prompt", (1, 1, TP, NH, HD)), ("av_prompt", (1, 1, TP, NH, HD)),
           ("bk_prompt", (1, 1, P, 2, HD)), ("bv_prompt", (1, 1, P, 2, HD)),
           ("ak_sample", (1, NS, 1, NH, HD)), ("av_sample", (1, NS, 1, NH, HD)),
           ("bk_sample", (1, NS, 1, 2, HD)), ("bv_sample", (1, NS, 1, 2, HD))]


def t5_bucket(n):
    exact = 16
    nf = np.maximum(n, 1).astype(np.float32)
    large = exact + (np.log(nf / np.float32(exact)) / np.float32(math.log(2048 / exact))
                     * np.float32(16)).astype(np.int32)
    return np.where(n < exact, n, np.minimum(large, 31))


EXT = 3 * P
STEPS_OF = (1, 4, 16, 1)


def constants():
    hot = np.zeros((33, 4, EXT), np.float32)
    for kind, step in enumerate(STEPS_OF):
        for j in range(EXT):
            dist = 255 - j
            if 0 <= dist <= P:
                hot[t5_bucket(np.array(dist * step)), kind, j] = 8.0
            else:
                hot[32, kind, j] = 8.0 * NEG
    rows = np.arange(NS * NH)
    who = np.concatenate([rows[:, None] // NH == np.arange(NS), rows[:, None] % NH == np.arange(NH),
                          rows[:, None] % NH // 4 == np.arange(2)], 1).astype(np.float32)
    return {"const_hot": hot, "const_who": who}


def build(nc, io):
    ctx = ExitStack()
    with ctx:
        arena = Arena(nc)

        def sem(name):
            return ctx.enter_context(nc.semaphore(name))

        def dram(name, shape):
            return nc.dram_tensor(name, shape, F32, kind="Internal").ap()

        off = 0
        Y = arena.at("Y", [P, KT, T], F32, off); off += 4 * KT * T
        HOFF = off
        Hhi = arena.at("Hhi", [P, KT, T], F32R, off); off += 4 * KT * T
        Hlo = arena.at("Hlo", [P, KT, T], F32R, off); off += 4 * KT * T
        WOFF = off
        Whi, Wlo = [], []
        wbytes = 4 * KT * P

        def weight_slot(o):
            s = len(Whi)
            Whi.append(arena.at(f"Whi{s}", [P, KT, P], F32R, o))
            Wlo.append(arena.at(f"Wlo{s}", [P, KT, P], F32R, o + wbytes))
            return o + 2 * wbytes

        off = weight_slot(weight_slot(off))
        RAW = []
        for i in range(3):
            RAW.append(arena.at(f"RAW{i}", [P, KT, P], F32, off)); off += wbytes
        ident = arena.at("ident", [P, P], F32, off); off += 4 * P
        meanw = arena.at("meanw", [P, P], F32, off); off += 4 * P
        modT = arena.at("modT", [P, MT, NC1], F32, off); off += 4 * MT * NC1
        vecT = arena.at("vecT", [P, MT + 6 * KT], F32, off); off += 4 * (MT + 6 * KT)
        siluT = arena.at("siluT", [P, KT, 32], F32, off); off += 4 * KT * 32
        modrow = arena.at("modrow", [96, 2 * P], F32, off); off += 4 * 2 * P
        A9 = arena.at("A9", [P, KT, NC1], F32, off); off += 4 * KT * NC1
        B9 = arena.at("B9", [P, KT, NC1], F32, off); off += 4 * KT * NC1
        G9 = arena.at("G9", [P, KT, NC1], F32, off); off += 4 * KT * NC1
        yS = arena.at("yS", [P, KT, NS], F32, off); off += 4 * KT * NS
        yv = arena.at("yv", [P, 2, KT], F32, off); off += 4 * 2 * KT
        epst = arena.at("epst", [P, 8], F32, off); off += 32
        off = up32(off)
        BIG = off
        projT = arena.at("projT", [P, PT, T], F32, BIG)
        PROJ_END = BIG + up32(4 * PT * T)
        SIL, GF = [], []
        for i in range(2):
            SIL.append(arena.at(f"SIL{i}", [P, TG], F32, off)); off += up32(4 * TG)
        for i in range(2):
            GF.append(arena.at(f"GF{i}", [P, TG], F32, off)); off += up32(4 * TG)
        Ghi, Glo = [], []
        for j in range(2):
            Ghi.append(arena.at(f"Ghi{j}", [P, T], F32R, off)); off += 4 * T
            Glo.append(arena.at(f"Glo{j}", [P, T], F32R, off)); off += 4 * T
        for s in range(4):
            off = weight_slot(off)
        LNOFF = off
        ADA = []
        o = LNOFF
        for i in range(3):
            ADA.append(arena.at(f"ADA{i}", [P, KT, 2 * P], F32, o)); o += 4 * KT * 2 * P
        o = LNOFF
        NT = []
        for i in range(2):
            NT.append(arena.at(f"NT{i}", [P, KT, TG], F32, o)); o += 4 * KT * TG
        RSTD = []
        for g in range(NG):
            RSTD.append(arena.at(f"RSTD{g}", [P, TG], F32, o)); o += up32(4 * TG)
        SQ = arena.at("SQ", [P, KT, T], F32, HOFF + 4 * KT * T)
        XTOK = arena.at("XTOK", [P, TB, D], F32, HOFF)
        XSMP = arena.at("XSMP", [NS, D], F32, HOFF + 4 * TB * D)
        VROW = arena.at("VROW", [MT + 6 * KT, P], F32, HOFF + 4 * TB * D + 4 * D)
        CROW = arena.at("CROW", [NC1 * KT, P], F32, HOFF + 4 * TB * D + 4 * D + 4 * P)
        OUTT = [arena.at(f"OUTT{i}", [P, D], F32, HOFF + 4 * D * i) for i in range(4)]

        OUTS = arena.at("OUTS", [NS, D], F32, HOFF + 16 * D)

        psum = ctx.enter_context(nc.psum_tensor("psum", [P, 8, 512], F32))
        bank = [psum[:, i, :] for i in range(8)]
        MISC = 7

        def group(g):
            return slice(g * TG, (g + 1) * TG)

        def mm3(pe, out, whi, wlo, xhi, xlo, first, last):
            pe.matmul(out, whi, xhi, start=first, stop=False)
            pe.matmul(out, whi, xlo, start=False, stop=False)
            return pe.matmul(out, wlo, xhi, start=False, stop=last)

        rows_in, x_in, const_ready = sem("rows_in"), sem("x_in"), sem("const_ready")
        setup_pe, setup_act, setup_dve = sem("setup_pe"), sem("setup_act"), sem("setup_dve")
        ada_in = [sem(f"ada_in{i}") for i in range(3)]
        ada_done, ada_evac, ada_turned = sem("ada_done"), sem("ada_evac"), sem("ada_turned")
        mod_prep = sem("mod_prep")
        raw_in = [sem(f"raw_in{i}") for i in range(3)]
        out_stored = sem("out_stored")

        class Stream:

            def __init__(self, name):
                self.hi, self.ready = sem(name + "_w_hi"), sem(name + "_w_ready")

        class FFN:
            def __init__(self, n):
                self.n = n
                self.w = Stream(f"ffn{n}")
                self.up_done, self.down_done = sem(f"ffn{n}_up_done"), sem(f"ffn{n}_down_done")
                self.silu_done, self.gf_done = sem(f"ffn{n}_silu_done"), sem(f"ffn{n}_gf_done")
                self.g_hi, self.g_ready = sem(f"ffn{n}_g_hi"), sem(f"ffn{n}_g_ready")
                self.y_evac = sem(f"ffn{n}_y_evac")
                names = [f"ffn{n}_wg", f"ffn{n}_wu", f"ffn{n}_wd"]
                g, u, d = (io[x][0] for x in names)
                self.wg, self.wu = (x.rearrange("(k p) n -> p k n", p=P) for x in (g, u))
                self.wd = d

            def source(self, f, s):
                j = s // 2 if s < 4 else s - 4
                if s < 4:
                    return (self.wg, self.wu)[s % 2][:, :, bass.ds((f + j) * P, P)]
                return self.wd[bass.ds((f + j) * P, P), :].rearrange("p (k n) -> p k n", k=KT)

        ffn = {1: FFN(1), 2: FFN(2)}
        W = {"ffn1": ffn[1].w, "proj": Stream("proj"), "wout": Stream("wout"), "ffn2": ffn[2].w}
        PIECES = {"ffn1": 6 * CH, "proj": PT, "wout": KT, "ffn2": 6 * CH}
        RAW_BEFORE, count = {}, [0, 0, 0]
        for name in ("ffn1", "proj", "wout", "ffn2"):
            RAW_BEFORE[name] = list(count)
            ring = 3 if name.startswith("ffn") else 2
            for i in range(ring):
                count[i] += PIECES[name] // ring
        ORDER = ["ffn1", "proj", "wout", "ffn2"]

        proj_done, proj_evac = sem("proj_done"), sem("proj_evac")
        wout_done, wout_evac = sem("wout_done"), sem("wout_evac")

        ln_mean, ln_centered, ln_squared, ln_var = (sem(x) for x in ("ln_mean", "ln_centered", "ln_squared", "ln_var"))
        ln_std, ln_rstd, ln_scaled, ln_hi = (sem(x) for x in ("ln_std", "ln_rstd", "ln_scaled", "ln_hi"))
        ln_lo, ln_y, ln_small, ln_shifted = (sem(x) for x in ("ln_lo", "ln_y", "ln_small", "ln_shifted"))
        resid_done = sem("resid_done")

        class Norm:

            def __init__(self, i):
                self.i, self.norm, self.mod = i, i > 0, i < 3

            def at(self, g):
                return NG * self.i + g + 1

            def n_at(self, g):
                return NG * (self.i - 1) + g + 1

            def half_at(self, g, half):
                return 2 * (NG * self.i + g) + half + 1

        init = Norm(0)
        ln = {i: Norm(i) for i in (1, 2, 3)}
        MEAN_BANK, VAR_BANK = (0, 1, 2), (7, 6, 5)
        INPUT = {"ffn1": init, "proj": ln[1], "ffn2": ln[2]}

        block = ctx.enter_context(nc.Block())

        def fetch(sp, phase, src, q, raw, use):
            sp.wait_ge(W[phase].ready, q + 1)
            sp.dma_start(RAW[raw][:, :, :], src).then_inc(raw_in[raw], 16)

        def split_hi(act, phase, slot, raw, use):
            act.wait_ge(raw_in[raw], use * 16 + 16 * (RAW_BEFORE[phase][raw] + 1))
            act.activation(Whi[slot][:, :, :], RAW[raw][:, :, :], ACT.Copy).then_inc(W[phase].hi, 1)

        def split_lo(pool, phase, slot, raw, q):
            pool.wait_ge(W[phase].hi, q + 1)
            pool.tensor_tensor(Wlo[slot][:, :, :], RAW[raw][:, :, :], Whi[slot][:, :, :].bitcast(F32),
                               ALU.subtract).then_inc(W[phase].ready, 1)

        def after_phase(sp, phase):
            i = ORDER.index(phase)
            if i:
                before = ORDER[i - 1]
                ring = 3 if before.startswith("ffn") else 2
                sp.wait_ge(W[before].ready, PIECES[before] + ring)

        def ffn_fetch_chunk(sp, x, c):
            for s in range(6):
                fetch(sp, f"ffn{x.n}", x.source(2 * c, s), 6 * c + s, s % 3, 2 * c + s // 3)

        def ffn_slot_free(eng, x, c, s):
            if s < 4:
                eng.wait_ge(x.up_done, 6 * c + 3 * (s // 2 + 1))
            else:
                eng.wait_ge(x.down_done, UNIT_D * c + UNIT_D)

        def ffn_split_hi(act, x, c, s):
            ffn_slot_free(act, x, c, s)
            split_hi(act, f"ffn{x.n}", s, s % 3, 2 * c + s // 3)

        def ffn_split_lo(pool, x, c, s):
            split_lo(pool, f"ffn{x.n}", s, s % 3, 6 * c + s)

        def ffn_pe(pe, x, c, ada=None, norm=None):
            for j in range(2):
                for g in range(NG):
                    u = 3 * j + g
                    gate, up = bank[2 * (u % 2)], bank[2 * (u % 2) + 1]
                    if g == 0:
                        pe.wait_ge(x.w.ready, 6 * c + 3 + 2 * (j + 1))
                    if j == 0:
                        pe.wait_ge(ln_lo, INPUT[f"ffn{x.n}"].half_at(g, 1))
                    pe.wait_ge(x.gf_done, 6 * c + u + 1)
                    for bk, s in ((gate, 2 * j), (up, 2 * j + 1)):
                        for k in range(KT):
                            last = mm3(pe, bk[:, 0:TG], Whi[s][:, k, :], Wlo[s][:, k, :],
                                       Hhi[:, k, group(g)], Hlo[:, k, group(g)], k == 0, k == KT - 1)
                    last.then_inc(x.up_done, 1)
            if ada is not None:
                ada_pe(pe, ada)
            pe.wait_ge(x.w.ready, 6 * c + 3 + 6)
            for g in range(NG):
                pe.wait_ge(x.g_ready, 6 * c + g + 6)
                for d in range(KT):
                    v = KT * g + d
                    bk = bank[4 + v % 3]
                    pe.wait_ge(x.y_evac, UNIT_D * c + v + 1)
                    for j in range(2):
                        last = mm3(pe, bk[:, 0:TG], Whi[4 + j][:, d, :], Wlo[4 + j][:, d, :],
                                   Ghi[j][:, group(g)], Glo[j][:, group(g)], j == 0, j == 1)
                    last.then_inc(x.down_done, 1)
                if ada is not None and g == 0:
                    ada_turn_pe(pe, ada)
                if norm is not None and g:
                    pe.wait_ge(x.y_evac, UNIT_D * (CH - 1) + KT * g + 3)
                    mean_pe(pe, norm, g - 1)

        def ffn_act(act, x, c, more):
            for u in range(6):
                act.wait_ge(x.up_done, 6 * c + u + 7)
                act.wait_ge(x.gf_done, 6 * c + u + 1)
                act.activation(SIL[u % 2][:, :], bank[2 * (u % 2)][:, 0:TG], ACT.Silu).then_inc(x.silu_done, 1)
                act.wait_ge(x.down_done, UNIT_D * c + KT * (u % 3 + 1))
                act.wait_ge(x.gf_done, 6 * c + u + 3)
                act.activation(Ghi[u // 3][:, group(u % 3)], GF[u % 2][:, :], ACT.Copy).then_inc(x.g_hi, 1)
                if more and u == 2:
                    for s in (0, 1):
                        ffn_split_hi(act, x, c + 1, s)
            if more:
                for s in range(2, 6):
                    ffn_split_hi(act, x, c + 1, s)

        def ffn_dve(dve, x, c, ada=None, before=None, norm=None):
            for u in range(6):
                if before is not None and u < NG:
                    norm_y(dve, before, u)
                dve.wait_ge(x.silu_done, 6 * c + u + 1)
                dve.wait_ge(x.g_ready, 6 * c + u + 1)
                dve.tensor_tensor(GF[u % 2][:, :], SIL[u % 2][:, :], bank[2 * (u % 2) + 1][:, 0:TG],
                                  ALU.mult).then_inc(x.gf_done, 1)
            if ada is not None:
                ada_dve(dve, ada)
            if before is not None:
                dve.wait_ge(ln_y, before.at(NG - 1))
            for g in range(NG):
                for d in range(KT):
                    v = KT * g + d
                    bk = bank[4 + v % 3]
                    n = TG if g < NG - 1 else PG
                    cols = slice(g * TG, g * TG + n)
                    dve.wait_ge(x.down_done, UNIT_D * c + v + UNIT_D + 1)
                    last = dve.scalar_tensor_tensor(Y[:, d, cols], bk[:, 0:n], G9[:, d, 0:1], Y[:, d, cols],
                                                    ALU.mult, ALU.add)
                    if g == NG - 1:
                        last = dve.tensor_tensor(yS[:, d, :], yS[:, d, :], bk[:, PG:TG], ALU.add)
                    last.then_inc(x.y_evac, 1)
                if ada is not None and g == 0:
                    ada_turn_dve(dve, ada)
                if norm is not None and g == 1:
                    center(dve, norm, 0)

        def ffn_pool(pool, x, c, more):
            for u in range(6):
                j, g = u // 3, u % 3
                pool.wait_ge(x.g_hi, 6 * c + u + 1)
                pool.tensor_tensor(Glo[j][:, group(g)], GF[u % 2][:, :], Ghi[j][:, group(g)].bitcast(F32),
                                   ALU.subtract).then_inc(x.g_ready, 1)
                if more and u == 2:
                    for s in (0, 1):
                        ffn_split_lo(pool, x, c + 1, s)
            if more:
                for s in range(2, 6):
                    ffn_split_lo(pool, x, c + 1, s)

        ADA_FIRST = 4
        ADA_ALL = MT // 6
        wada = io["w_ada"][0].rearrange("(k p) n -> p k n", p=P)

        def ada_fetch(sp, m):
            for i in range(3):
                sp.wait_ge(ada_done, m + 1)
                sp.dma_start(ADA[i][:, :, :], wada[:, :, bass.ds((6 * m + 2 * i) * P, 2 * P)]).then_inc(ada_in[i], 16)

        def ada_pe(pe, m):
            pe.wait_ge(ada_evac, 2 * m + 1)
            for i in range(3):
                pe.wait_ge(ada_in[i], 16 * m + 16)
                for k in range(KT):
                    last = pe.matmul(bank[MISC][32 * i:32 * i + 32, 0:2 * P], siluT[:, k, :], ADA[i][:, k, :],
                                     start=(k == 0), stop=(k == KT - 1))
            last.then_inc(ada_done, 1)

        def ada_turn_pe(pe, m):
            pe.wait_ge(ada_evac, 2 * m + 2)
            for j in range(2):
                last = pe.transpose(bank[MISC][:, 96 * j:96 * j + 96], modrow[:, j * P:(j + 1) * P],
                                    ident[0:96, 0:96])
            last.then_inc(ada_turned, 1)

        def ada_dve(dve, m):
            dve.wait_ge(ada_done, m + 2)
            dve.tensor_copy(modrow[:, :], bank[MISC][0:96, 0:2 * P]).then_inc(ada_evac, 1)

        def ada_turn_dve(dve, m):
            dve.wait_ge(ada_turned, m + 1)
            for j in range(2):
                bias = vecT[:, bass.ds(6 * m + j, 3, step=2)].unsqueeze(2).to_broadcast([P, 3, NC1])
                last = dve.tensor_tensor(modT[:, bass.ds(6 * m + j, 3, step=2), :],
                                         bank[MISC][:, 96 * j:96 * j + 96].rearrange("p (i n) -> p i n", n=32)[:, :, 0:NC1],
                                         bias, ALU.add)
            last.then_inc(ada_evac, 1)

        def mod(i):
            return modT[:, i * KT:(i + 1) * KT, :]

        def lnv(what, i):
            o = MT + (3 * KT if what == "b" else 0) + i * KT
            return vecT[:, o:o + KT]

        prep_steps = [0]

        def prep(dve, shift, scale, norm, last_norm=False):
            def step(ins):
                prep_steps[0] += 1
                ins.then_inc(mod_prep, 1)
                dve.wait_ge(mod_prep, prep_steps[0])

            if scale is not None:
                step(dve.tensor_scalar(A9[:, :, :], mod(scale), 1.0, None, ALU.add))
            if norm is None:
                step(dve.tensor_copy(B9[:, :, :], mod(shift)))
                return
            g, b = lnv("g", norm), lnv("b", norm)
            if scale is not None:
                step(dve.tensor_tensor(B9[:, :, :], A9[:, :, :], b.unsqueeze(2).to_broadcast([P, KT, NC1]), ALU.mult))
                step(dve.tensor_tensor(B9[:, :, :], B9[:, :, :], mod(shift), ALU.add))
                step(dve.tensor_tensor(A9[:, :, :], A9[:, :, :], g.unsqueeze(2).to_broadcast([P, KT, NC1]), ALU.mult))
            a = 1.0 if last_norm else ALPHA
            step(dve.tensor_scalar(yv[:, 0, :], g, a, None, ALU.mult))
            step(dve.tensor_scalar(yv[:, 1, :], b, a, None, ALU.mult))

        def prep_gate(dve, which, factor):
            for ins in (lambda: dve.tensor_scalar(G9[:, :, :], mod(which), factor, None, ALU.mult),
                        lambda: dve.memset(yS[:, :, :], 0.0)):
                prep_steps[0] += 1
                ins().then_inc(mod_prep, 1)
                dve.wait_ge(mod_prep, prep_steps[0])

        def samples_in(dve):
            for ins in (lambda: dve.tensor_tensor(yS[:, :, :], yS[:, :, :], G9[:, :, 1:], ALU.mult),
                        lambda: dve.tensor_tensor(Y[:, :, TP:], Y[:, :, TP:], yS[:, :, :], ALU.add)):
                prep_steps[0] += 1
                ins().then_inc(mod_prep, 1)
                dve.wait_ge(mod_prep, prep_steps[0])

        def sum_pe(pe, out, src):
            for k in range(KT):
                last = pe.matmul(out, meanw[:, :], src(k), start=(k == 0), stop=(k == KT - 1))
            return last

        def mean_pe(pe, n, g):
            sum_pe(pe, bank[MEAN_BANK[g]][:, 0:TG], lambda k: Y[:, k, group(g)]).then_inc(ln_mean, 1)

        def var_pe(pe, n, g):
            pe.wait_ge(ln_squared, n.n_at(g))
            sum_pe(pe, bank[VAR_BANK[g]][:, 0:TG], lambda k: SQ[:, k, group(g)]).then_inc(ln_var, 1)

        def norm_pe(pe, n):
            pe.wait_ge(resid_done, n.i)
            if n.i == 2:
                mean_pe(pe, n, 0)
                mean_pe(pe, n, 1)
            var_pe(pe, n, 0)
            mean_pe(pe, n, 2)
            var_pe(pe, n, 1)
            var_pe(pe, n, 2)

        def center(dve, n, g):
            y = Y[:, :, group(g)]
            dve.wait_ge(ln_mean, n.n_at(g))
            mean = bank[MEAN_BANK[g]][:, 0:TG].unsqueeze(1).to_broadcast([P, KT, TG])
            dve.tensor_tensor(y, y, mean, ALU.subtract).then_inc(ln_centered, 1)

        small_steps = [0]

        def scaled(dve, n, g):
            def step(ins):
                small_steps[0] += 1
                ins.then_inc(ln_small, 1)
                dve.wait_ge(ln_small, small_steps[0])

            cols = PG if g == NG - 1 and n.mod else TG
            own = slice(g * TG, g * TG + cols)
            if n.norm:
                dve.wait_ge(ln_std, n.n_at(g))
                dve.reciprocal(RSTD[g][:, :], RSTD[g][:, :]).then_inc(ln_rstd, 1)
                dve.wait_ge(ln_rstd, n.n_at(g))
                dve.wait_ge(ln_centered, n.n_at(g))
            if n.mod and g == 2:
                dve.wait_ge(ln_lo, n.half_at(0, 1))
            if n.mod and g == NG - 1:
                ys, ts = Y[:, :, TP:], NT[g % 2][:, :, PG:]
                if n.norm:
                    step(dve.tensor_tensor(ts, ys, RSTD[g][:, PG:].unsqueeze(1).to_broadcast([P, KT, NS]), ALU.mult))
                    step(dve.tensor_tensor(ts, ts, A9[:, :, 1:], ALU.mult))
                else:
                    step(dve.tensor_tensor(ts, ys, A9[:, :, 1:], ALU.mult))
                step(dve.tensor_tensor(ts, ts, B9[:, :, 1:], ALU.add))
            for k in range(KT):
                out = NT[g % 2][:, k, 0:cols] if n.mod else Y[:, k, own]
                gain = A9[:, k, 0:1] if n.mod else yv[:, 0, k:k + 1]
                if n.norm:
                    last = dve.scalar_tensor_tensor(out, Y[:, k, own], gain, RSTD[g][:, 0:cols], ALU.mult, ALU.mult)
                else:
                    last = dve.tensor_scalar(out, Y[:, k, own], gain, None, ALU.mult)
                if k % 4 == 3:
                    last.then_inc(ln_scaled, 1)

        def norm_dve(dve, n):
            if n.norm:
                center(dve, n, 1)
                scaled(dve, n, 0)
                center(dve, n, 2)
                scaled(dve, n, 1)
                scaled(dve, n, 2)
            else:
                for g in range(NG):
                    scaled(dve, n, g)

        def norm_y(dve, n, g):
            dve.wait_ge(ln_scaled, n.half_at(g, 1))
            y = Y[:, :, group(g)]
            if not n.norm:
                dve.tensor_scalar(y, y, ALPHA, None, ALU.mult).then_inc(ln_y, 1)
                return
            for k in range(KT):
                y = Y[:, k, group(g)]
                last = dve.scalar_tensor_tensor(y, y, yv[:, 0, k:k + 1], RSTD[g][:, :], ALU.mult, ALU.mult)
            small_steps[0] += 1
            last.then_inc(ln_small, 1)
            dve.wait_ge(ln_small, small_steps[0])
            for k in range(KT):
                y = Y[:, k, group(g)]
                last = dve.tensor_scalar(y, y, yv[:, 1, k:k + 1], None, ALU.add)
            last.then_inc(ln_y, 1)

        def square(act, n, g):
            act.wait_ge(ln_centered, n.n_at(g))
            act.activation(SQ[:, :, group(g)], Y[:, :, group(g)], ACT.Square).then_inc(ln_squared, 1)

        def std(act, n, g):
            act.wait_ge(ln_var, n.n_at(g))
            act.activation(RSTD[g][:, :], bank[VAR_BANK[g]][:, 0:TG], ACT.Sqrt, bias=epst[:, 0:1]).then_inc(ln_std, 1)

        def shifted_hi(act, n, g):
            cols = PG if g == NG - 1 and n.mod else TG
            own = slice(g * TG, g * TG + cols)
            for k in range(KT):
                if k % 4 == 0:
                    act.wait_ge(ln_scaled, n.half_at(g, k // 4))
                src = NT[g % 2][:, k, 0:cols] if n.mod else Y[:, k, own]
                dst = Hhi[:, k, own] if n.mod else Y[:, k, own]
                last = act.activation(dst, src, ACT.Identity, bias=B9[:, k, 0:1] if n.mod else yv[:, 1, k:k + 1])
                if n.mod and g == NG - 1 and k % 4 == 3:
                    last = act.activation(Hhi[:, k - 3:k + 1, TP:], NT[g % 2][:, k - 3:k + 1, PG:], ACT.Copy)
                if k % 4 == 3:
                    last.then_inc(ln_hi, 1)

        def norm_act(act, n):
            if n.norm:
                square(act, n, 0)
                square(act, n, 1)
                std(act, n, 0)
                shifted_hi(act, n, 0)
                square(act, n, 2)
            for g in range(NG):
                if n.norm and g:
                    std(act, n, g)
                if g or not n.norm:
                    shifted_hi(act, n, g)

        def norm_pool(pool, n):
            for g in range(NG):
                cols = PG if g == NG - 1 else TG
                own = slice(g * TG, g * TG + cols)
                for half in range(2):
                    ks = slice(4 * half, 4 * half + 4)
                    pool.wait_ge(ln_scaled, n.half_at(g, half))
                    pool.tensor_tensor(SQ[:, ks, own], NT[g % 2][:, ks, 0:cols],
                                       B9[:, ks, 0:1].to_broadcast([P, 4, cols]), ALU.add).then_inc(ln_shifted, 1)
                    pool.wait_ge(ln_hi, n.half_at(g, half))
                    pool.wait_ge(ln_shifted, n.half_at(g, half))
                    last = pool.tensor_tensor(Hlo[:, ks, own], SQ[:, ks, own], Hhi[:, ks, own].bitcast(F32),
                                              ALU.subtract)
                    if g == NG - 1:
                        last = pool.tensor_tensor(Hlo[:, ks, TP:], NT[g % 2][:, ks, PG:], Hhi[:, ks, TP:].bitcast(F32),
                                                  ALU.subtract)
                    last.then_inc(ln_lo, 1)

        win = io["w_in"][0].rearrange("(k p) n -> p k n", p=P)

        def pair_fetch(sp, phase, source, i):
            for j in range(2):
                fetch(sp, phase, source(2 * i + j), 2 * i + j, j, i)

        def pair_split_hi(act, phase, done, i, j):
            if done is not None:
                act.wait_ge(done, NG * (2 * i + j) - NG)
            split_hi(act, phase, j, j, i)

        def pair_pe(pe, phase, done, evac, i, h_numbers, h_sem):
            for j in range(2):
                pe.wait_ge(W[phase].ready, 2 * i + j + 3)
                for g in range(NG):
                    pe.wait_ge(h_sem, h_numbers[g])
                    u = NG * j + g
                    pe.wait_ge(evac, 6 * i + u + 1)
                    for k in range(KT):
                        last = mm3(pe, bank[u][:, 0:TG], Whi[j][:, k, :], Wlo[j][:, k, :],
                                   Hhi[:, k, group(g)], Hlo[:, k, group(g)], k == 0, k == KT - 1)
                    last.then_inc(done, 1)

        def proj_source(t):
            return win[:, :, bass.ds(t * P, P)]

        def proj_act(act, i, more):
            for j in range(2):
                for g in range(NG):
                    act.wait_ge(proj_done, 6 * i + NG * j + g + 1)
                    act.activation(projT[:, bass.ds(2 * i + j, 1), group(g)], bank[NG * j + g][:, 0:TG],
                                   ACT.Copy).then_inc(proj_evac, 1)
                if more:
                    pair_split_hi(act, "proj", proj_done, i + 1, j)

        wout = io["w_out"][0].rearrange("(k p) n -> p k n", p=P)

        def wout_source(t):
            return wout[:, :, bass.ds(t * P, P)]

        out_ready, out_pe, out_act = sem("out_ready"), sem("out_pe"), sem("out_act")
        out_slot = [sem(f"out_slot{i}") for i in range(4)]

        OUT_BANKS = ((3, 4), (0, 1))

        def wout_dve(dve, i):
            for j in range(2):
                for g in range(NG):
                    n = TG if g < NG - 1 else PG
                    d, cols = 2 * i + j, slice(g * TG, g * TG + n)
                    bk = bank[NG * j + g]
                    dve.wait_ge(wout_done, 6 * i + NG * j + g + 1)
                    last = dve.scalar_tensor_tensor(Y[:, d, cols], bk[:, 0:n], G9[:, d, 0:1], Y[:, d, cols],
                                                    ALU.mult, ALU.add)
                    if g == NG - 1:
                        last = dve.tensor_tensor(yS[:, d, :], yS[:, d, :], bk[:, PG:TG], ALU.add)
                    last.then_inc(wout_evac, 1)

        SCALE = HD ** -0.5
        bias_rows = [dram(f"bias_rows{k}", (P, NH * EXT)) for k in range(4)]
        o = HOFF + 4 * TB * D + 4 * D + 8 * P
        BST = [arena.at(f"BST{i}", [P, NH, EXT], F32, o + 4 * NH * EXT * i) for i in range(2)]
        assert o + 8 * NH * EXT <= HOFF + 8 * KT * T
        HOT = arena.at("HOT", [33, 4, EXT], F32, BIG)
        REL = arena.at("REL", [33, 2 * NH], F32, BIG + 4 * 4 * EXT)
        RELX = arena.at("RELX", [33, 2 * NH, P], F32, BIG + 4 * 4 * EXT + 64)
        rel_in, rel_x, bias_mm, bias_ev, one_set = (sem(x) for x in ("rel_in", "rel_x", "bias_mm", "bias_ev", "one_set"))
        bias_st = [sem(f"bias_st{i}") for i in range(2)]

        AUG = HD + 1
        RW = NH * AUG + NH
        MAXO = NH * AUG
        o = HOFF
        VT = arena.at("VT", [P, TB, 10, AUG], F32, o); o += 4 * TB * 10 * AUG
        V4 = arena.at("V4", [P, TB, NH, AUG], F32, o); o += 4 * TB * NH * AUG
        V16 = arena.at("V16", [P, TB, NH, AUG], F32, o); o += 4 * TB * NH * AUG
        qS = []
        for i in range(2):
            qS.append(arena.at(f"qS{i}", [P, 4, P], F32, o)); o += 4 * 4 * P
        REC = []
        for i in range(2):
            REC.append(arena.at(f"REC{i}", [P, RW], F32, o)); o += up32(4 * RW)
        small = arena.at("small", [P, 8, 3 * NH], F32, o); o += 4 * 8 * 3 * NH
        MAXR = arena.at("MAXR", [P, 4, 4], F32, o); o += 64
        parts = arena.at("parts", [P, 2], F32, o); o += 32
        sinkb = arena.at("sinkb", [P, NH], F32, o); o += 4 * NH
        assert o <= HOFF + 8 * KT * T, o - HOFF - 8 * KT * T
        SS = [arena.at(f"SS{i}", [P, 4, 2 * P], F32, WOFF + 4096 * i) for i in range(2)]
        PTB = [arena.at(f"PTB{i}", [P, 4, 2, P], F32, WOFF + 8192 + 4096 * i) for i in range(2)]
        o = BIG + 4 * T * TVA
        BIASB = arena.at("BIASB", [P, NH, 2 * P], F32, o)
        BIAS1 = arena.at("BIAS1", [P, NH, 2 * P], F32, o + 8192)
        MIX = arena.at("MIX", [P, D], F32, BIG + 4 * T * TVB)
        o = PROJ_END
        BIAS4 = arena.at("BIAS4", [P, NH, 2 * P], F32, o); o += 8192
        kB2 = arena.at("kB2", [P, TP], F32, o); o += 4096
        BIAS16 = arena.at("BIAS16", [P, NH, P], F32, PROJ_END + 13312)
        MR = arena.at("MR", [P, 3, RW], F32, WOFF + 16384)
        KST = [arena.at(f"KST{i}", [P, 10 * HD], F32, PROJ_END + 2560 * i) for i in range(4)]
        RS = arena.at("RS", [NS, PT * P], F32, WOFF)
        assert 3 * RW * 4 <= 3 * wbytes and 4 * NS * 0 + 4 * PT * P <= 16384

        scr16, scr4 = dram("scr16", (TP, RW)), dram("scr4", (TP, RW))
        new_rows = dram("new_rows", (2, NS * NH))
        akp = io["ak_prompt"][0, 0].rearrange("t h d -> t (h d)")
        avp = io["av_prompt"][0, 0].rearrange("t h d -> t (h d)")
        av_heads = io["av_prompt"][0, 0]

        kv_turned, kv_evac, k_copied = sem("kv_turned"), sem("kv_evac"), sem("k_copied")
        k_stored = [sem(f"k_stored{i}") for i in range(4)]
        v_stored, v16_in, v4_in = sem("v_stored"), sem("v16_in"), sem("v4_in")
        b16_in, b4_in, b_in = sem("b16_in"), sem("b4_in"), sem("b_in")
        q_staged, qk_done, max_done, sub_done, exp_done = (sem(x) for x in (
            "q_staged", "qk_done", "max_done", "sub_done", "exp_done"))
        t_done, t_evac, pv_done, o_evac = sem("t_done"), sem("t_evac"), sem("pv_done"), sem("o_evac")
        rec_stored = [sem(f"rec_stored{i}") for i in range(2)]
        branch_in, merge_step, merge_exp = sem("branch_in"), sem("merge_step"), sem("merge_exp")
        parts_set, max_begun = sem("parts_set"), sem("max_begun")
        mix_split_hi, mix_split, ones_set = sem("mix_split_hi"), sem("mix_split"), sem("ones_set")
        MIX_READY = [1, 2, 3]

        class Half:
            H = {"L": 2, "M": 4, "N": 4}
            COUNT = {"L": 8, "M": 4, "N": 8}
            BASE = {"L": 0, "M": 16, "N": 32}
            NEXT = {"L": "M", "M": "N"}
            BEFORE = {"M": "L", "N": "M"}

            def __init__(self, phase, i, l, even=None, half_i=None):
                self.phase, self.i, self.l = phase, i, l
                self.even = i % 2 == 0 if even is None else even
                self.half_i = i // 2 if half_i is None else half_i

            def step(self, n):
                h = self.H[self.phase]
                di, l = (self.l + n) // h, (self.l + n) % h
                i = self.i + di
                if isinstance(i, int) and i >= self.COUNT[self.phase]:
                    if self.phase == "N":
                        return None
                    return Half(self.NEXT[self.phase], 0, 0).step((i - self.COUNT[self.phase]) * h + l)
                if isinstance(i, int) and i < 0:
                    if self.phase == "L":
                        return None
                    b = self.BEFORE[self.phase]
                    return Half(b, self.COUNT[b] - 1, self.H[b] - 1).step(i * h + l + 1)
                if isinstance(i, int):
                    return Half(self.phase, i, l)
                even = self.even == (di % 2 == 0)
                half_i = self.half_i + (di // 2 if self.even else (di + 1) // 2)
                return Half(self.phase, i, l, even, half_i)

            @property
            def x(self):
                return self.BASE[self.phase] + self.H[self.phase] * self.i + self.l

            @property
            def y(self):
                if self.phase != "N" or (isinstance(self.i, int) and self.i == 0):
                    return self.x
                return 36 + 5 * (self.i - 1) + self.l + (self.l >= 2)

            @property
            def hh(self):
                return self.l % 2

            @property
            def parity(self):
                return self.l % 2

            @property
            def is_b(self):
                return self.phase == "N" and self.l < 2

            @property
            def blocks(self):
                if self.phase == "L":
                    return 1
                if self.phase == "M":
                    return 1 + self.l // 2
                return 1 if isinstance(self.i, int) and self.i == 0 else 2

            def columns(self, tile, keys):
                nb = self.blocks if keys else 1
                if self.phase == "L":
                    return tile.rearrange("p (j r) -> p r j", r=16)[:, bass.ds(2 * self.i, 2), :]
                if self.phase == "M":
                    b = self.l // 2
                    first = b + 1 - nb
                    return tile.rearrange("p (j r) -> p r j", r=4)[:, bass.ds(self.i, 1), first * P:(first + nb) * P]
                return tile[:, bass.ds((self.i + 1 - nb) * P, nb * P)]

            def bias(self, h):
                n = self.blocks * P
                if self.phase == "L":
                    return BIAS16[:, h, :]
                table = BIAS4 if self.phase == "M" else BIASB if self.is_b else BIAS1
                return table[:, h, 2 * P - n:2 * P]

            def values(self, h, kb):
                if self.phase == "L":
                    return V16[:, bass.ds(self.i, 1), h, :]
                if self.phase == "M":
                    return V4[:, bass.ds(2 * self.i + self.l // 2 + 1 - self.blocks + kb, 1), h, :]
                return VT[:, bass.ds(self.i + 1 - self.blocks + kb, 1), 8 + h // 4 if self.is_b else h, :]

            @property
            def record(self):
                if self.phase == "N" and not self.is_b:
                    return MR[:, 0, :]
                return REC[self.unit_parity][:, :]

            @property
            def maxima(self):
                slot = self.l if self.H[self.phase] == 4 else self.l + (0 if self.even else 2)
                return MAXR[:, slot, :]

            @property
            def unit_parity(self):
                if self.phase == "M":
                    return self.l // 2
                return 0 if self.even else 1

        def drive(eng, body, phase):
            n, h = Half.COUNT[phase], Half.H[phase]
            edge = 1 if phase == "M" else 2

            def block_of(i, even=None, half_i=None):
                for l in range(h):
                    body(Half(phase, i, l, even, half_i))

            for i in range(edge):
                block_of(i)
            if phase == "M":
                with eng.Fori(edge, n - edge) as i:
                    block_of(i, True, i)
            else:
                with eng.Fori(0, (n - 2 * edge) // 2) as ii:
                    block_of(2 * ii + edge, True, ii + 1)
                    block_of(2 * ii + edge + 1, False, ii + 1)
            for i in range(n - edge, n):
                block_of(i)

        def stage_q(pool, hf):
            if hf is None:
                return
            pool.wait_ge(qk_done, hf.x + 1)
            tile = (TQB if hf.is_b else TQA) + 2 * hf.hh
            mask = parts[:, :].unsqueeze(2).unsqueeze(3)
            for t in range(2):
                src = hf.columns(projT[:, tile + t, 0:TP], False)
                if hf.phase != "L":
                    src = src if hf.phase == "M" else src.rearrange("p (r j) -> p r j", r=1)
                r, n = src.shape[1:]
                last = pool.tensor_tensor(qS[hf.parity][:, 2 * t:2 * t + 2, :].rearrange("p o (r j) -> p o r j", r=r),
                                          src.unsqueeze(1).to_broadcast([P, 2, r, n]),
                                          mask.to_broadcast([P, 2, r, n]), ALU.mult)
            last.then_inc(q_staged, 1)

        def scores_pe(pe, hf):
            if hf is None:
                return
            pe.wait_ge(q_staged, hf.x + 1)
            pe.wait_ge(max_done, hf.x + 1)
            if hf.is_b:
                pe.wait_ge(b_in, 16 * 5)
            n = hf.blocks * P
            for j in range(4):
                h = 4 * hf.hh + j
                if hf.is_b:
                    keys = projT[:, TKB, 0:TP] if h % 2 == h // 4 else kB2[:, :]
                else:
                    keys = projT[:, TKA + h // 2, 0:TP]
                last = pe.matmul(bank[2 * hf.parity + j % 2][:, (j // 2) * 2 * P:(j // 2) * 2 * P + n],
                                 qS[hf.parity][:, j, :], hf.columns(keys, True),
                                 start=True, stop=True)
            last.then_inc(qk_done, 1)

        def max_dve(dve, hf):
            if hf is None:
                return
            dve.wait_ge(qk_done, hf.x + 3)
            if hf.step(-2) is not None:
                dve.wait_ge(t_done, hf.step(-2).y + 3)
            if hf.step(-4) is not None:
                dve.wait_ge(o_evac, hf.step(-4).x + 3)
            n = hf.blocks * P
            if hf.phase == "L":
                dve.wait_ge(b16_in, 32)
            elif hf.phase == "M":
                dve.wait_ge(b4_in, 16)
            else:
                dve.wait_ge(b_in, 16 * 5)
            dve.sem_inc(max_begun, 1)
            for j in range(4):
                h = 4 * hf.hh + j
                last = dve.tensor_tensor_reduce(
                    SS[hf.parity][:, j, 0:n],
                    bank[2 * hf.parity + j % 2][:, (j // 2) * 2 * P:(j // 2) * 2 * P + n], hf.bias(h),
                    SCALE, sinkb[:, h:h + 1] if hf.is_b else -3.0e38, ALU.add, ALU.max,
                    hf.maxima[:, j:j + 1])
            last.then_inc(max_done, 1)

        def sub_pool(pool, hf):
            if hf is None:
                return
            pool.wait_ge(max_done, hf.x + 3)
            n = hf.blocks * P
            s = SS[hf.parity][:, :, 0:n]
            m = hf.maxima.unsqueeze(2).to_broadcast([P, 4, n])
            pool.tensor_tensor(s, s, m, ALU.subtract).then_inc(sub_done, 1)

        def exp_act(act, hf):
            if hf is None:
                return
            act.wait_ge(sub_done, hf.x + 1)
            s = SS[hf.parity][:, :, 0:hf.blocks * P]
            act.activation(s, s, ACT.Exp).then_inc(exp_done, 1)

        def turn_pe(pe, hf):
            pe.wait_ge(exp_done, hf.x + 1)
            pe.wait_ge(t_evac, hf.y + 1)
            for j in range(4):
                for kb in range(hf.blocks):
                    c = (j % 2) * 2 * P + kb * P
                    last = pe.transpose(bank[4 + j // 2][:, c:c + P], SS[hf.parity][:, j, kb * P:(kb + 1) * P],
                                        ident[:, :])
            last.then_inc(t_done, 1)

        def turn_act(act, hf):
            act.wait_ge(t_done, hf.y + 3)
            act.wait_ge(pv_done, hf.x + 1)
            nb = hf.blocks
            src = psum[:, 4:6, :].rearrange("p a (j k q) -> p (a j) k q", j=2, k=2)[:, :, 0:nb, :]
            act.activation(PTB[hf.parity][:, :, 0:nb, :], src, ACT.Copy).then_inc(t_evac, 1)

        def values_pe(pe, hf):
            if hf is None:
                return
            pe.wait_ge(t_evac, hf.y + 2)
            pe.wait_ge(o_evac, hf.x + 1)
            nb = hf.blocks
            for j in range(4):
                for kb in range(nb):
                    last = pe.matmul(bank[6 + hf.parity][:, j * AUG:(j + 1) * AUG], PTB[hf.parity][:, j, kb, :],
                                     hf.values(4 * hf.hh + j, kb), start=(kb == 0), stop=(kb == nb - 1))
            last.then_inc(pv_done, 1)

        def values_dve(dve, hf):
            if hf is None:
                return
            if hf.hh == 0:
                if hf.phase == "L":
                    if not (isinstance(hf.i, int) and hf.i < 2):
                        dve.wait_ge(rec_stored[hf.unit_parity], 32 * hf.half_i)
                elif hf.phase == "M":
                    dve.wait_ge(rec_stored[hf.unit_parity], 128 + 16 * hf.i)
                elif isinstance(hf.i, int) and hf.i < 2 and hf.is_b:
                    dve.wait_ge(rec_stored[hf.unit_parity], 192)
            dve.wait_ge(pv_done, hf.x + 3)
            c = 4 * hf.hh * AUG
            m = MAXO + 4 * hf.hh
            dve.tensor_copy(hf.record[:, c:c + 4 * AUG], bank[6 + hf.parity][:, 0:4 * AUG])
            dve.tensor_copy(hf.record[:, m:m + 4], hf.maxima).then_inc(o_evac, 1)

        STEPS_B, STEPS_A = 4, 9

        def merge_at(b, what, n):
            return (STEPS_A + STEPS_B) * b + (STEPS_B if what == "a" else 0) + n

        def mix_y(b):
            return 71 if isinstance(b, int) and b == TB - 1 else 36 + 5 * b + 2

        def small_of(n, w):
            return small[:, n, 0:w]

        def merge_b_dve(dve, hf):
            b, rec = hf.i, hf.record
            recs = rec[:, 0:MAXO].rearrange("p (h a) -> p h a", a=AUG)
            n = [0]

            def step(ins):
                n[0] += 1
                ins.then_inc(merge_step, 1)
                dve.wait_ge(merge_step, merge_at(b, "b", n[0]))

            dve.wait_ge(o_evac, hf.x + 3)
            step(dve.tensor_tensor(small_of(0, NH), sinkb[:, :], rec[:, MAXO:MAXO + NH], ALU.subtract))
            dve.wait_ge(merge_exp, 2 * b + 1)
            step(dve.tensor_tensor(small_of(2, NH), small_of(1, NH), recs[:, :, HD], ALU.add))
            step(dve.reciprocal(small_of(3, NH), small_of(2, NH)))
            if not (isinstance(b, int) and b == 0):
                dve.wait_ge(t_done, mix_y(b - 1) + 3)
            step(dve.tensor_tensor(MIX[:, NH * HD:].rearrange("p (h a) -> p h a", a=HD), recs[:, :, 0:HD],
                                   small_of(3, NH).unsqueeze(2).to_broadcast([P, NH, HD]), ALU.mult))

        def merge_a_dve(dve, hf):
            b = hf.i
            outs = MR[:, :, 0:MAXO].rearrange("p s (h a) -> p s h a", a=AUG)
            maxima = MR[:, :, MAXO:MAXO + NH]
            n = [0]

            def step(ins):
                n[0] += 1
                ins.then_inc(merge_step, 1)
                dve.wait_ge(merge_step, merge_at(b, "a", n[0]))

            def three(i):
                return small[:, i, :].rearrange("p (s h) -> p s h", s=3)

            dve.wait_ge(o_evac, hf.x + 3)
            dve.wait_ge(branch_in, 32 * b + 32)
            step(dve.tensor_reduce(small_of(4, NH), maxima.rearrange("p s h -> p h s"), AXX, ALU.max))
            step(dve.tensor_tensor(three(5), maxima, small_of(4, NH).unsqueeze(1).to_broadcast([P, 3, NH]),
                                   ALU.subtract))
            dve.wait_ge(merge_exp, 2 * b + 2)
            step(dve.tensor_tensor(three(7), three(6), outs[:, :, :, HD], ALU.mult))
            step(dve.tensor_reduce(small_of(4, NH), three(7).rearrange("p s h -> p h s"), AXX, ALU.add))
            step(dve.reciprocal(small_of(4, NH), small_of(4, NH)))
            step(dve.tensor_tensor(three(7), three(6), small_of(4, NH).unsqueeze(1).to_broadcast([P, 3, NH]),
                                   ALU.mult))
            for s in range(3):
                last = dve.tensor_tensor(outs[:, s, :, 0:HD], outs[:, s, :, 0:HD],
                                         small[:, 7, s * NH:(s + 1) * NH].unsqueeze(2).to_broadcast([P, NH, HD]),
                                         ALU.mult)
            step(last)
            mix = MIX[:, 0:NH * HD].rearrange("p (h a) -> p h a", a=HD)
            step(dve.tensor_tensor(mix, outs[:, 0, :, 0:HD], outs[:, 1, :, 0:HD], ALU.add))
            step(dve.tensor_tensor(mix, mix, outs[:, 2, :, 0:HD], ALU.add))

        def merge_exp_act(act, hf):
            if hf.is_b:
                act.wait_ge(merge_step, merge_at(hf.i, "b", 1))
                act.activation(small_of(1, NH), small_of(0, NH), ACT.Exp).then_inc(merge_exp, 1)
            else:
                act.wait_ge(merge_step, merge_at(hf.i, "a", 2))
                act.activation(small_of(6, 3 * NH), small_of(5, 3 * NH), ACT.Exp).then_inc(merge_exp, 1)

        def mix_pe(pe, b):
            pe.wait_ge(merge_step, merge_at(b, "a", STEPS_A))
            pe.wait_ge(t_evac, mix_y(b) + 1)
            for t in range(KT):
                last = pe.transpose(bank[4 + t // 4][:, (t % 4) * P:(t % 4 + 1) * P], MIX[:, t * P:(t + 1) * P],
                                    ident[:, :])
            last.then_inc(t_done, 1)

        def mix_act(act, b):
            act.wait_ge(t_done, mix_y(b) + 3)
            for half, tile in enumerate((TQA, TQB)):
                last = act.activation(projT[:, tile:tile + 4, bass.ds(b * P, P)],
                                      bank[4 + half].rearrange("p (t q) -> p t q", q=P), ACT.Copy)
            last.then_inc(t_evac, 1)

        def mix_due(hf):
            return hf.phase == "N" and hf.l == 2 and not (isinstance(hf.i, int) and hf.i == 0)

        def merge_due(hf):
            return hf is not None and hf.phase == "N" and hf.l % 2 == 1

        def attn_pe(pe, hf):
            if mix_due(hf):
                mix_pe(pe, hf.i - 1)
            scores_pe(pe, hf.step(2))
            turn_pe(pe, hf)
            values_pe(pe, hf.step(-1))

        def attn_act(act, hf):
            if mix_due(hf):
                mix_act(act, hf.i - 1)
            turn_act(act, hf)
            exp_act(act, hf.step(2))
            if merge_due(hf.step(-1)):
                merge_exp_act(act, hf.step(-1))

        def attn_dve(dve, hf):
            before = hf.step(-1)
            values_dve(dve, before)
            max_dve(dve, hf.step(2))
            if merge_due(before):
                (merge_b_dve if before.is_b else merge_a_dve)(dve, before)

        def attn_pool(pool, hf):
            stage_q(pool, hf.step(3))
            sub_pool(pool, hf.step(2))

        LAST = Half("N", TB - 1, 3)

        def attn_sp(sp, hf):
            if hf.phase == "N":
                if hf.l == 0:
                    if not (isinstance(hf.i, int) and hf.i == 0):
                        sp.wait_ge(merge_step, merge_at(hf.i - 1, "a", STEPS_A))
                    for s, scr in ((1, scr4), (2, scr16)):
                        sp.dma_start(MR[:, s, :], scr[bass.ds(hf.i * P, P), :]).then_inc(branch_in, 16)
                return
            if hf.hh == 1:
                sp.wait_ge(o_evac, hf.x + 3)
                if hf.phase == "L":
                    rows = scr16.rearrange("(j r) c -> r j c", r=16)
                    for rr in range(2):
                        sp.dma_start(rows[bass.ds(2 * hf.i + rr, 1), :, :],
                                     REC[hf.unit_parity][HD * rr:HD * rr + HD, :]).then_inc(
                                         rec_stored[hf.unit_parity], 16)
                else:
                    rows = scr4.rearrange("(b p r) c -> r b p c", r=4, p=P)
                    sp.dma_start(rows[bass.ds(hf.i, 1), hf.l // 2, :, :], REC[hf.l // 2][:, :]).then_inc(
                        rec_stored[hf.l // 2], 16)

        def kv_pe(pe, b):
            if b:
                pe.wait_ge(kv_evac, 2 * b)
            for which, tiles in enumerate((list(range(TKA, TKA + 4)) + [TKB], list(range(TVA, TVA + 4)) + [TVB])):
                for n, t in enumerate(tiles):
                    last = pe.transpose(bank[2 * which + n // 4][:, (n % 4) * P:(n % 4 + 1) * P],
                                        projT[:, t, b * P:(b + 1) * P], ident[:, :])
            last.then_inc(kv_turned, 1)

        def kv_act(act, b):
            act.wait_ge(kv_turned, b + 1)
            if b >= 4:
                act.wait_ge(k_stored[b % 4], 16)
            act.activation(KST[b % 4][:, 0:512], bank[0], ACT.Copy)
            act.activation(KST[b % 4][:, 512:640], bank[1][:, 0:P], ACT.Copy).then_inc(kv_evac, 1)

        def kv_dve(dve, b):
            dve.wait_ge(kv_evac, 2 * b + 1)
            dve.tensor_copy(VT[:, b, 0:NH, 0:HD], bank[2].rearrange("p (h a) -> p h a", a=HD))
            dve.tensor_copy(VT[:, b, NH:, 0:HD], bank[3][:, 0:P].rearrange("p (h a) -> p h a", a=HD)).then_inc(kv_evac, 1)

        def kv_sp(sp, b):
            sp.wait_ge(kv_evac, 2 * b + 2)
            sp.dma_start(akp[b * P:(b + 1) * P, :], KST[b % 4][:, 0:512]).then_inc(k_stored[b % 4], 16)
            sp.dma_start(av_heads[b * P:(b + 1) * P, :, :], VT[:, b, 0:NH, 0:HD]).then_inc(v_stored, 16)
            if b == TB - 1:
                sp.dma_start(io["bk_prompt"][0, 0].rearrange("t h d -> t (h d)"), KST[3][:, 512:640]).then_inc(out_stored, 16)
                sp.dma_start(io["bv_prompt"][0, 0], VT[:, b, NH:, 0:HD]).then_inc(out_stored, 16)

        def tables_sp(sp):
            sp.wait_ge(v_stored, 16 * TB)
            v16 = av_heads.rearrange("(j r) h d -> r j h d", r=16)
            for u in range(TB):
                for rr in range(2):
                    sp.dma_start(V16[HD * rr:HD * rr + HD, u, :, 0:HD], v16[2 * u + rr]).then_inc(v16_in, 16)
            first, row = P - 1 + P, NH * EXT - 1
            sp.dma_start(BIAS16[0:HD, :, :], bass.AP(bias_rows[2].tensor, first, [[row, HD], [EXT, NH], [1, P]])).then_inc(b16_in, 16)
            sp.dma_start(BIAS16[HD:, :, HD:], bass.AP(bias_rows[2].tensor, first + HD * row + HD,
                                                      [[row, HD], [EXT, NH], [1, HD]])).then_inc(b16_in, 16)
            v4 = av_heads.rearrange("(b p r) h d -> r b p h d", r=4, p=P)
            for r in range(4):
                for b in range(2):
                    sp.dma_start(V4[:, 2 * r + b, :, 0:HD], v4[r, b]).then_inc(v4_in, 16)

        def late_tables_sp(sp):
            sp.wait_ge(samp_done, 1)
            def skew(k):
                return bass.AP(bias_rows[k].tensor, P - 1, [[NH * EXT - 1, P], [EXT, NH], [1, 2 * P]])

            sp.dma_start(BIAS4[:, :, :], skew(1)).then_inc(b4_in, 16)
            sp.dma_start(BIAS1[:, :, :], skew(0)).then_inc(b_in, 16)
            sp.dma_start(BIASB[:, :, :], skew(3)).then_inc(b_in, 16)
            sp.dma_start(sinkb[:, :], bass.AP(io["sinks"].tensor, 0, [[0, P], [1, NH]])).then_inc(b_in, 16)
            for half in range(2):
                sp.dma_start(kB2[HD * half:HD * half + HD, :],
                             projT[HD * (1 - half):HD * (1 - half) + HD, TKB, 0:TP]).then_inc(b_in, 16)

        KC = 3 * NH * HD + 2 * HD
        tail = HOFF + 4 * TB * (10 + 2 * NH) * AUG
        SK = [arena.at("SK0", [P, KC], F32, WOFF + 4 * PT * P), arena.at("SK1", [P, KC], F32, WOFF + 4 * PT * P + 4 * KC),
              arena.at("SK2", [P, KC], F32, tail)]
        PRDB = [arena.at(f"PRDB{i}", [P, NH, HD], F32, tail + 4 * KC + 2048 * i) for i in range(2)]
        assert tail + 4 * KC + 4096 <= HOFF + 8 * KT * T
        o = WOFF + 4 * PT * P + 8 * KC
        QA = [arena.at("QA0", [P, NH * HD], F32, o), arena.at("QA1", [P, NH * HD], F32, o + 4096)]
        QB = [arena.at("QB0", [P, NH * HD], F32, o + 2048), arena.at("QB1", [P, NH * HD], F32, PROJ_END + 11264)]
        assert o + 6144 <= WOFF + 7 * wbytes
        ROWS = NS * NH
        sT = arena.at("sT", [P, 4, NS, NH], F32, PROJ_END + 10240)
        o = BIG + 4 * T * TVA
        SR = arena.at("SR", [ROWS, 4, P + 1], F32, o); o += up32(16 * (P + 1))
        SBIAS = arena.at("SBIAS", [ROWS, 4, P + 1], F32, o); o += up32(16 * (P + 1))
        SV1 = arena.at("SV1", [ROWS, 64], F32, o); o += 256
        NEW = arena.at("NEW", [NS, 2, NH, HD], F32, o); o += 4 * 2 * NH * HD
        SNEWT = arena.at("SNEWT", [NS, 2, NH], F32, o); o += 4 * 2 * NH
        o = PROJ_END
        PZ = arena.at("PZ", [P, NS, 4, ROWS], F32, o); o += 4 * NS * 4 * ROWS
        PN = arena.at("PN", [NS, 2, ROWS], F32, o); o += 8 * ROWS
        MA = arena.at("MA", [ROWS, NH, HD], F32, o); o += 4 * NH * HD
        MB = arena.at("MB", [ROWS, NH, HD], F32, o); o += 4 * NH * HD
        o = BIG + 4 * T * TVB
        OBG = arena.at("OBG", [ROWS, 2, HD], F32, o)
        OBS = arena.at("OBS", [ROWS, HD], F32, o + 512)
        DN = arena.at("DN", [ROWS, 2, NS], F32, o + 768)
        who = arena.at("who", [ROWS, NS + NH + 2], F32, o + 832)
        MAX_, NEGM, DEN, RDEN, PNEW, SNEW = (slice(2 * i, 2 * i + 2) for i in (0, 1, 2, 3, 4, 7))
        SINK, SINK8, ESINK = (slice(i, i + 1) for i in (11, 12, 13))
        samp_pe, samp_act, samp_dve = sem("samp_pe"), sem("samp_act"), sem("samp_dve")
        samp_done, new_out, new_in = (sem(x) for x in ("samp_done", "new_out", "new_in"))
        q_spread, q_copied, prd_own = sem("q_spread"), sem("q_copied"), sem("prd_own")
        samp_in = [sem(f"samp_in{i}") for i in range(3)]
        sampv_in = [sem(f"sampv_in{i}") for i in range(3)]
        BY_DVE = (2, 5)
        samp_tables = sem("samp_tables")
        prd_done, red_done, sampv_done = sem("prd_done"), sem("red_done"), sem("sampv_done")

        def cache_rows(name, n, step):
            rows = io[name][0, n].rearrange("(p s) h d -> p s (h d)", s=step)
            return rows[rows.shape[0] - P:, 0, :]

        def samp_load(sp, what, n, slot, signal):
            for s, step in enumerate((1, 4, 16)):
                sp.dma_start(SK[slot][:, s * 512:(s + 1) * 512], cache_rows(f"cache_a_{what}", n, step)).then_inc(signal, 16)
            sp.dma_start(SK[slot][:, 1536:], cache_rows(f"cache_b_{what}", n, 1)).then_inc(signal, 16)

        def keys_sp(sp, n):
            if n >= 3:
                sp.wait_ge(red_done, n - 2)
            samp_load(sp, "k", n, n % 3, samp_in[n % 3])

        def samp_values_sp(sp, n):
            if n < 3:
                sp.wait_ge(red_done, max(m for m in range(NS) if m % 3 == n) + 1)
            else:
                sp.wait_ge(sampv_done, n - 2)
            samp_load(sp, "v", n, n % 3, sampv_in[n % 3])

        def samp_outs_sp(sp):
            sp.wait_ge(samp_dve, samp_at["rows"])
            for name, t, w in (("ak_sample", TKA, 4), ("av_sample", TVA, 4), ("bk_sample", TKB, 1), ("bv_sample", TVB, 1)):
                sp.dma_start(io[name][0].rearrange("n t h d -> (n t) (h d)"), RS[:, t * P:(t + w) * P]).then_inc(out_stored, 16)

        def samp_tables_sp(sp):
            sp.wait_ge(kv_turned, TB)
            sp.dma_start(who[:, :], io["const_who"]).then_inc(samp_tables, 16)
            sp.dma_start(SV1[:, SINK], bass.AP(io["sinks"].tensor, 0, [[0, NS], [1, NH], [1, 1]])).then_inc(samp_tables, 16)
            for k in range(4):
                sp.dma_start(SBIAS[:, k, :], bass.AP(bias_rows[k].tensor, P - 1, [[EXT, ROWS], [1, P + 1]])).then_inc(samp_tables, 16)

        def samp_new_sp(sp):
            sp.wait_ge(samp_dve, samp_at["new"])
            sp.dma_start(new_rows.rearrange("a (n h) -> n a h", h=NH), SNEWT[:, :, :]).then_inc(new_out, 16)
            sp.wait_ge(new_out, 16)
            for a in range(2):
                sp.dma_start(SV1[:, 14 + a:15 + a], bass.AP(new_rows.tensor, a * ROWS, [[1, ROWS], [1, 1]])).then_inc(new_in, 16)

        def samp_products(eng, n):
            slot = n % 3
            eng.wait_ge(samp_in[slot], 64 * (n // 3 + 1))
            eng.wait_ge(q_copied, n + 1)
            if n >= 2:
                eng.wait_ge(red_done, n - 1)
            k = SK[slot][:, 0:1536].rearrange("p (s c) -> p s c", s=3)
            eng.tensor_tensor(k, k, QA[n % 2][:, :].unsqueeze(1).to_broadcast([P, 3, NH * HD]), ALU.mult)
            k = SK[slot][:, 1536:].rearrange("p (g d) -> p g d", g=2)
            for g in range(2):
                last = eng.tensor_tensor(PRDB[n % 2][:, 4 * g:4 * g + 4, :],
                                         QB[n % 2][:, 256 * g:256 * g + 256].rearrange("p (h d) -> p h d", h=4),
                                         k[:, g:g + 1, :].to_broadcast([P, 4, HD]), ALU.mult)
            last.then_inc(prd_own if n in BY_DVE else prd_done, 1)

        def samp_prod_pool(pool):
            for n in range(NS):
                if n not in BY_DVE:
                    samp_products(pool, n)

        def samp_sum_dve(dve, n):
            if n in BY_DVE:
                samp_products(dve, n)
                dve.wait_ge(prd_own, BY_DVE.index(n) + 1)
            else:
                dve.wait_ge(prd_done, n + 1 - sum(m < n for m in BY_DVE))
            dve.tensor_reduce(sT[:, 0:3, n, :], SK[n % 3][:, 0:1536].rearrange("p (s h d) -> p s h d", s=3, h=NH),
                              AXX, ALU.add)
            dve.tensor_reduce(sT[:, 3, n, :], PRDB[n % 2][:, :, :], AXX, ALU.add).then_inc(red_done, 1)

        def spread_pe(pe, n):
            if n >= 2:
                pe.wait_ge(q_copied, n - 1)
            one = ident[0:NS, n:n + 1].to_broadcast([NS, P])
            pe.matmul(bank[4 + 2 * (n % 2)], one, RS[:, TQA * P:(TQA + 4) * P], start=True, stop=True)
            pe.matmul(bank[5 + 2 * (n % 2)], one, RS[:, TQB * P:(TQB + 4) * P], start=True, stop=True).then_inc(q_spread, 1)

        def spread_act(act, n):
            act.wait_ge(q_spread, n + 1)
            if n >= 2:
                act.wait_ge(red_done, n - 1)
            act.activation(QA[n % 2][:, :], bank[4 + 2 * (n % 2)], ACT.Copy)
            act.activation(QB[n % 2][:, :], bank[5 + 2 * (n % 2)], ACT.Copy).then_inc(q_copied, 1)

        def samp_rows_pe(pe):
            for t in range(PT):
                last = pe.transpose(bank[t // 4][0:NS, (t % 4) * P:(t % 4 + 1) * P], projT[:, t, TP:], ident[:, :])
            last.then_inc(samp_pe, 1)

        def samp_pe_run(pe):
            pe.wait_ge(red_done, NS)
            for s in range(4):
                last = pe.transpose(bank[0][0:ROWS, s * P:(s + 1) * P], sT[:, s, :, :].rearrange("p n h -> p (n h)"), ident[:, :])
            last.then_inc(samp_pe, 1)
            pe.wait_ge(samp_dve, samp_at["d"])
            for s in range(4):
                pe.transpose(bank[1][:, s * ROWS:(s + 1) * ROWS], SR[:, s, 0:P], ident[0:ROWS, 0:ROWS])
            for a in range(2):
                last = pe.transpose(bank[2][0:NS, a * ROWS:(a + 1) * ROWS], DN[:, a, :], ident[0:ROWS, 0:ROWS])
            last.then_inc(samp_pe, 1)
            pe.wait_ge(samp_dve, samp_at["pz"])
            oa, ob = bank[3][0:ROWS, :], bank[4][0:ROWS, 0:2 * HD]
            for n in range(NS):
                slot = n % 3
                pe.wait_ge(sampv_in[slot], 64 * (n // 3 + 1))
                for s in range(3):
                    pe.matmul(oa, PZ[:, n, s, :], SK[slot][:, s * 512:(s + 1) * 512], start=(n == 0 and s == 0), stop=False)
                pe.matmul(ob, PZ[:, n, 3, :], SK[slot][:, 1536:], start=(n == 0), stop=False).then_inc(sampv_done, 1)
            pe.matmul(oa, PN[:, 0, :], RS[:, TVA * P:(TVA + 4) * P], start=False, stop=True)
            pe.matmul(ob, PN[:, 1, :], RS[:, TVB * P:(TVB + 1) * P], start=False, stop=True).then_inc(samp_pe, 1)
            pe.wait_ge(samp_dve, samp_at["mb"])
            for t in range(KT):
                src = (MA if t < 4 else MB)[:, 2 * (t % 4):2 * (t % 4) + 2, :].rearrange("p h d -> p (h d)")
                last = pe.matmul(bank[5][:, t * NS:(t + 1) * NS], src, who[:, 0:NS], start=True, stop=True)
            last.then_inc(samp_pe, 1)

        samp_at = Numbers(["rows", "new_mul", "new", "pz0", "bias", "newc", "max_a", "max_b", "sink8", "max_bs", "negm",
                           "den", "rden", "p_a", "p_b", "pnew_a", "pnew_b", "d_a", "d", "pz", "ma", "obg", "obs", "mb",
                           "out"])

        def samp_dve_run(dve):
            def step(name, ins):
                ins.then_inc(samp_dve, 1)
                dve.wait_ge(samp_dve, samp_at[name])

            dve.wait_ge(samp_pe, 1)
            for k in range(5):
                w = 512 if k < 4 else 256
                last = dve.tensor_copy(RS[:, k * 512:k * 512 + w], bank[k][0:NS, 0:w])
            step("rows", last)
            for n in range(NS):
                kv_dve(dve, n)
                samp_sum_dve(dve, n)
            dve.wait_ge(kv_turned, TB)
            heads = RS[:, :].rearrange("p (h d) -> p h d", d=HD)
            dve.tensor_tensor(NEW[:, 0, :, :], heads[:, 0:8, :], heads[:, 8:16, :], ALU.mult)
            for g in range(2):
                last = dve.tensor_tensor(NEW[:, 1, 4 * g:4 * g + 4, :], heads[:, 24 + 4 * g:28 + 4 * g, :],
                                         heads[:, 32 + g:33 + g, :].to_broadcast([NS, 4, HD]), ALU.mult)
            step("new_mul", last)
            step("new", dve.tensor_reduce(SNEWT[:, :, :], NEW[:, :, :, :], AXX, ALU.add))
            for b in range(4):
                dve.wait_ge(k_stored[b], 32)
            dve.wait_ge(out_stored, 16 * 6)
            step("pz0", dve.memset(PZ[:, :, :, :], 0.0))
            dve.wait_ge(samp_pe, 2)
            dve.wait_ge(samp_tables, 16 * 6)
            step("bias", dve.tensor_tensor(SR[:, :, 0:P], bank[0][0:ROWS, :].rearrange("p (s k) -> p s k", s=4),
                                           SBIAS[:, :, 0:P], ALU.add))
            dve.wait_ge(new_in, 32)
            dve.tensor_tensor(SR[:, 0:3, P:], SBIAS[:, 0:3, P:], SV1[:, 14:15].unsqueeze(1).to_broadcast([ROWS, 3, 1]), ALU.add)
            step("newc", dve.tensor_tensor(SR[:, 3, P:], SBIAS[:, 3, P:], SV1[:, 15:16], ALU.add))
            step("max_a", dve.tensor_reduce(SV1[:, 0:1], SR[:, 0:3, :].rearrange("p s k -> p (s k)"), AXX, ALU.max))
            step("max_b", dve.tensor_reduce(SV1[:, 1:2], SR[:, 3, :], AXX, ALU.max))
            step("sink8", dve.tensor_scalar(SV1[:, SINK8], SV1[:, SINK], 1.0 / SCALE, None, ALU.mult))
            step("max_bs", dve.tensor_tensor(SV1[:, 1:2], SV1[:, 1:2], SV1[:, SINK8], ALU.max))
            step("negm", dve.tensor_scalar(SV1[:, NEGM], SV1[:, MAX_], -SCALE, None, ALU.mult))
            dve.wait_ge(samp_act, 1)
            step("den", dve.tensor_tensor(SV1[:, 5:6], SV1[:, 5:6], SV1[:, ESINK], ALU.add))
            step("rden", dve.reciprocal(SV1[:, RDEN], SV1[:, DEN]))
            step("p_a", dve.tensor_scalar(SR[:, 0:3, :], SR[:, 0:3, :], SV1[:, 6:7], None, ALU.mult))
            step("p_b", dve.tensor_scalar(SR[:, 3, :], SR[:, 3, :], SV1[:, 7:8], None, ALU.mult))
            step("pnew_a", dve.tensor_reduce(SV1[:, 8:9], SR[:, 0:3, P], AXX, ALU.add))
            step("pnew_b", dve.tensor_copy(SV1[:, 9:10], SR[:, 3, P:]))
            step("d_a", dve.tensor_scalar(DN[:, 0, :], who[:, 0:NS], SV1[:, 8:9], None, ALU.mult))
            step("d", dve.tensor_scalar(DN[:, 1, :], who[:, 0:NS], SV1[:, 9:10], None, ALU.mult))
            dve.wait_ge(samp_pe, 3)
            pz = PZ[:, :, :, :]
            diag = bass.AP(pz.tensor, pz.offset, [list(pz.ap[0]), [4 * ROWS + NH, NS], [ROWS, 4], [1, NH]])
            dve.tensor_copy(diag, bank[1][:, 0:4 * ROWS].rearrange("p (s n h) -> p n s h", s=4, h=NH))
            step("pz", dve.tensor_copy(PN[:, :, :], bank[2][0:NS, 0:2 * ROWS].rearrange("p (a r) -> p a r", a=2)))
            dve.wait_ge(samp_pe, 4)
            own = who[:, NS:NS + NH].unsqueeze(2).to_broadcast([ROWS, NH, HD])
            step("ma", dve.tensor_tensor(MA[:, :, :], bank[3][0:ROWS, :].rearrange("p (h d) -> p h d", d=HD), own, ALU.mult))
            step("obg", dve.tensor_tensor(OBG[:, :, :], bank[4][0:ROWS, 0:2 * HD].rearrange("p (g d) -> p g d", g=2),
                                          who[:, NS + NH:].unsqueeze(2).to_broadcast([ROWS, 2, HD]), ALU.mult))
            step("obs", dve.tensor_tensor(OBS[:, :], OBG[:, 0, :], OBG[:, 1, :], ALU.add))
            step("mb", dve.tensor_tensor(MB[:, :, :], OBS[:, :].unsqueeze(1).to_broadcast([ROWS, NH, HD]), own, ALU.mult))
            dve.wait_ge(samp_pe, 5)
            o5 = bank[5][:, 0:KT * NS].rearrange("p (t n) -> p t n", n=NS)
            dve.tensor_copy(projT[:, TQA:TQA + 4, TP:], o5[:, 0:4, :])
            step("out", dve.tensor_copy(projT[:, TQB:TQB + 4, TP:], o5[:, 4:8, :]))
            dve.sem_inc(samp_done, 1)

        def samp_act_run(act):
            act.wait_ge(samp_dve, samp_at["negm"])
            flat = SR[:, 0:3, :].rearrange("p s k -> p (s k)")
            act.activation(flat, flat, ACT.Exp, bias=SV1[:, 2:3], scale=SCALE, accum_out=SV1[:, 4:5])
            act.activation(SR[:, 3, :], SR[:, 3, :], ACT.Exp, bias=SV1[:, 3:4], scale=SCALE, accum_out=SV1[:, 5:6])
            act.activation(SV1[:, ESINK], SV1[:, SINK], ACT.Exp, bias=SV1[:, 3:4]).then_inc(samp_act, 1)


        def out_half(eng, b, half):
            rows = P if b < TB else NS
            dst = OUTT[b % 4] if b < TB else OUTS
            eng.wait_ge(out_pe, b + 1)
            if 4 <= b < TB:
                eng.wait_ge(out_slot[b % 4], 16 * (b // 4))
            src = bank[OUT_BANKS[b % 2][half]][0:rows, :]
            out = dst[0:rows, half * 512:(half + 1) * 512]
            if half:
                eng.activation(out, src, ACT.Copy).then_inc(out_act, 1)
            else:
                eng.wait_ge(out_act, b + 1)
                eng.tensor_copy(out, src).then_inc(out_ready, 1)

        @block.sync
        def _(sp):
            VA = VROW
            sp.dma_start(CROW[0:KT, :], io["c_prompt"].rearrange("n (k p) -> (n k) p", p=P)).then_inc(rows_in, 16)
            sp.dma_start(CROW[KT:, :], io["c_sample"].rearrange("n (k p) -> (n k) p", p=P)).then_inc(rows_in, 16)
            sp.dma_start(VA[0:MT, :], io["b_ada"].rearrange("l (k p) -> (l k) p", p=P)).then_inc(rows_in, 16)
            sp.dma_start(VA[MT:MT + 3 * KT, :], io["ln_g"].rearrange("l i (k p) -> (l i k) p", p=P)).then_inc(rows_in, 16)
            sp.dma_start(VA[MT + 3 * KT:, :], io["ln_b"].rearrange("l i (k p) -> (l i k) p", p=P)).then_inc(rows_in, 16)
            ada_fetch(sp, 0)
            sp.dma_start(XTOK[:, :, :], io["x_prompt"][0].rearrange("(b p) d -> p b d", p=P)).then_inc(x_in, 16)
            sp.dma_start(XSMP[:, :], io["x_sample"].rearrange("n t d -> (n t) d")).then_inc(x_in, 16)
            sp.dma_start(HOT[:, :, :], io["const_hot"]).then_inc(rel_in, 16)
            sp.wait_ge(one_set, 1)
            sp.dma_start(REL[0:32, :], io["rel_bias"]).then_inc(rel_in, 16)
            for k in range(4):
                sp.wait_ge(bias_ev, NH * (k + 1))
                sp.dma_start(bias_rows[k], BST[k % 2][:, :, :].rearrange("p h e -> p (h e)")).then_inc(bias_st[k % 2], 16)
            with sp.Fori(1, ADA_FIRST) as m:
                ada_fetch(sp, m)
            ffn_fetch_chunk(sp, ffn[1], 0)
            sp.wait_ge(ln_lo, init.half_at(NG - 1, 1))
            ada_fetch(sp, ADA_FIRST)
            with sp.Fori(0, ADA_ALL - ADA_FIRST - 1) as c:
                ffn_fetch_chunk(sp, ffn[1], c + 1)
                ada_fetch(sp, c + ADA_FIRST + 1)
            with sp.Fori(ADA_ALL - ADA_FIRST - 1, CH - 1) as c:
                ffn_fetch_chunk(sp, ffn[1], c + 1)
            after_phase(sp, "proj")
            with sp.Fori(0, PT // 2) as i:
                pair_fetch(sp, "proj", proj_source, i)
            sp.wait_ge(proj_done, NG * PT)
            sp.wait_ge(W["proj"].ready, PIECES["proj"] + 2)
            for n in range(3):
                keys_sp(sp, n)
            samp_outs_sp(sp)
            for b in range(TB):
                kv_sp(sp, b)
                if b + 3 < NS:
                    keys_sp(sp, b + 3)
            samp_tables_sp(sp)
            for n in range(3):
                samp_values_sp(sp, n)
            samp_new_sp(sp)
            tables_sp(sp)
            for n in range(3, NS):
                samp_values_sp(sp, n)
            late_tables_sp(sp)
            for phase in "LMN":
                if phase == "N":
                    for i in range(2):
                        sp.wait_ge(rec_stored[i], 192)
                drive(sp, lambda hf: attn_sp(sp, hf), phase)
            sp.wait_ge(merge_step, merge_at(TB - 1, "a", STEPS_A))
            after_phase(sp, "wout")
            with sp.Fori(0, KT // 2) as i:
                pair_fetch(sp, "wout", wout_source, i)
            after_phase(sp, "ffn2")
            with sp.Fori(0, CH) as c:
                ffn_fetch_chunk(sp, ffn[2], c)
            for b in range(TB):
                sp.wait_ge(out_ready, b + 1)
                sp.dma_start(io["y_prompt"][0, b * P:(b + 1) * P, :], OUTT[b % 4][:, :]).then_inc(out_slot[b % 4], 16)
            sp.wait_ge(out_ready, TB + 1)
            sp.dma_start(io["y_sample"].rearrange("n t d -> (n t) d"), OUTS[:, :]).then_inc(out_stored, 16)
            sp.wait_ge(out_stored, 16 * 7)
            for i in range(4):
                sp.wait_ge(out_slot[i], 16 * (TB // 4))

        @block.gpsimd
        def _(pool):
            pool.memset(ident[:, :], 0.0).then_inc(const_ready, 1)
            pool.wait_ge(const_ready, 1)
            pool.affine_select(out=ident[:, :], in_=ident[:, :], compare_op=ALU.not_equal, fill=1.0, base=0,
                               pattern=[[-1, P]], channel_multiplier=1).then_inc(const_ready, 1)
            pool.memset(meanw[:, :], 1.0 / D).then_inc(const_ready, 1)
            pool.memset(epst[:, :], EPS).then_inc(const_ready, 1)
            for name in ORDER:
                pool.sem_inc(W[name].ready, 3 if name.startswith("ffn") else 2)
            for n in (1, 2):
                pool.sem_inc(ffn[n].g_ready, 2)
            pool.memset(REL[:, :], 1.0).then_inc(one_set, 1)
            pool.sem_inc(t_evac, 1)
            for s in range(6):
                ffn_split_lo(pool, ffn[1], 0, s)
            norm_pool(pool, init)
            with pool.Fori(0, CH - 1) as c:
                ffn_pool(pool, ffn[1], c, True)
            ffn_pool(pool, ffn[1], CH - 1, False)
            for j in range(2):
                split_lo(pool, "proj", j, j, j)
            norm_pool(pool, ln[1])
            with pool.Fori(1, PT // 2) as i:
                for j in range(2):
                    split_lo(pool, "proj", j, j, 2 * i + j)
            pool.wait_ge(proj_done, NG * PT)
            pool.memset(VT[:, :, :, HD:], 1.0)
            pool.memset(V16[:, :, :, HD:], 1.0)
            pool.memset(V4[:, :, :, HD:], 1.0).then_inc(ones_set, 1)
            samp_prod_pool(pool)
            pool.wait_ge(parts_set, 1)
            for x in range(3):
                stage_q(pool, Half("L", 0, 0).step(x))
            for x in range(2):
                sub_pool(pool, Half("L", 0, 0).step(x))
            for phase in "LMN":
                drive(pool, lambda hf: attn_pool(pool, hf), phase)
            for g in range(NG):
                pool.wait_ge(mix_split_hi, g + 1)
                for half, tile in enumerate((TQA, TQB)):
                    last = pool.tensor_tensor(Hlo[:, 4 * half:4 * half + 4, group(g)], projT[:, tile:tile + 4, group(g)],
                                              Hhi[:, 4 * half:4 * half + 4, group(g)].bitcast(F32), ALU.subtract)
                last.then_inc(mix_split, 1)
            with pool.Fori(0, KT // 2) as i:
                for j in range(2):
                    split_lo(pool, "wout", j, j, 2 * i + j)
            for s in range(6):
                ffn_split_lo(pool, ffn[2], 0, s)
            norm_pool(pool, ln[2])
            with pool.Fori(0, CH - 1) as c:
                ffn_pool(pool, ffn[2], c, True)
            ffn_pool(pool, ffn[2], CH - 1, False)

        XU = TB // 4 * KT

        @block.scalar
        def _(act):
            act.wait_ge(setup_pe, 2)
            act.wait_ge(setup_dve, 1)
            act.activation(siluT[:, :, 0:NC1].rearrange("p k n -> p n k"),
                           bank[1][:, 0:NC1 * KT].rearrange("p (n k) -> p n k", k=KT), ACT.Silu).then_inc(setup_act, 1)
            for u in range(XU):
                act.wait_ge(setup_pe, 3 + u)
                k, h = u // 2, u % 2
                act.activation(Y[:, k, h * 512:(h + 1) * 512], bank[2 + u % 4][:, :], ACT.Copy).then_inc(setup_act, 1)
            act.wait_ge(setup_pe, 3 + XU)
            act.activation(Y[:, :, TP:], bank[6][:, 0:KT * NS].rearrange("p (k n) -> p k n", n=NS),
                           ACT.Copy).then_inc(setup_act, 1)
            for s in range(6):
                split_hi(act, "ffn1", s, s % 3, s // 3)
            norm_act(act, init)
            with act.Fori(0, CH - 1) as c:
                ffn_act(act, ffn[1], c, True)
            ffn_act(act, ffn[1], CH - 1, False)
            act.wait_ge(ffn[1].up_done, 6 * CH + 6)
            for j in range(2):
                pair_split_hi(act, "proj", None, 0, j)
            norm_act(act, ln[1])
            with act.Fori(0, PT // 2 - 1) as i:
                proj_act(act, i, True)
            proj_act(act, PT // 2 - 1, False)
            act.wait_ge(ln_y, ln[1].at(NG - 1))
            for n in range(2):
                spread_act(act, n)
            for b in range(TB):
                kv_act(act, b)
                if b + 2 < NS:
                    spread_act(act, b + 2)
            samp_act_run(act)
            for x in range(2):
                exp_act(act, Half("L", 0, 0).step(x))
            for phase in "LMN":
                drive(act, lambda hf: attn_act(act, hf), phase)
            merge_exp_act(act, LAST)
            mix_act(act, TB - 1)
            act.wait_ge(t_evac, 73)
            for g in range(NG):
                for half, tile in enumerate((TQA, TQB)):
                    last = act.activation(Hhi[:, 4 * half:4 * half + 4, group(g)], projT[:, tile:tile + 4, group(g)],
                                          ACT.Copy)
                last.then_inc(mix_split_hi, 1)
            for j in range(2):
                pair_split_hi(act, "wout", None, 0, j)
            with act.Fori(1, KT // 2) as i:
                for j in range(2):
                    pair_split_hi(act, "wout", wout_done, i, j)
            act.wait_ge(wout_done, NG * KT)
            for s in range(6):
                split_hi(act, "ffn2", s, s % 3, s // 3)
            norm_act(act, ln[2])
            with act.Fori(0, CH - 1) as c:
                ffn_act(act, ffn[2], c, True)
            ffn_act(act, ffn[2], CH - 1, False)
            act.wait_ge(ffn[2].up_done, 6 * CH + 6)
            norm_act(act, ln[3])
            for b in range(TB + 1):
                out_half(act, b, 1)

        @block.vector
        def _(dve):
            for n in (1, 2):
                dve.sem_inc(ffn[n].gf_done, 2)
                dve.sem_inc(ffn[n].y_evac, 3)
            dve.sem_inc(ada_evac, 1)
            for s in (max_done, o_evac):
                dve.sem_inc(s, 2)
            dve.sem_inc(proj_evac, 6)
            dve.sem_inc(wout_evac, 6)
            dve.memset(siluT[:, :, :], 0.0).then_inc(setup_dve, 1)
            dve.wait_ge(setup_pe, 1)
            dve.tensor_copy(vecT[:, :], bank[0][:, 0:MT + 6 * KT]).then_inc(setup_dve, 1)
            dve.wait_ge(setup_dve, 2)
            dve.wait_ge(rel_in, 32)
            dve.tensor_copy(RELX[:, :, :], REL[:, :].unsqueeze(2).to_broadcast([33, 2 * NH, P])).then_inc(rel_x, 1)
            for n in range(4 * NH):
                k, h = n // NH, n % NH
                if k >= 2 and h == 0:
                    dve.wait_ge(bias_st[k % 2], 16)
                dve.wait_ge(bias_mm, n + 1)
                dve.tensor_copy(BST[k % 2][:, h, :], bank[n % 2][:, 0:EXT]).then_inc(bias_ev, 1)
            for k in range(2):
                dve.wait_ge(bias_st[k], 32)
            with dve.Fori(0, ADA_FIRST) as m:
                ada_dve(dve, m)
                ada_turn_dve(dve, m)
            dve.wait_ge(ada_evac, 2 * ADA_FIRST + 1)
            prep(dve, 0, 1, None)
            prep_gate(dve, 2, 0.5)
            dve.wait_ge(setup_act, 2 + XU)
            norm_dve(dve, init)
            ffn_dve(dve, ffn[1], 0, ADA_FIRST, before=init)
            with dve.Fori(1, ADA_ALL - ADA_FIRST) as c:
                ffn_dve(dve, ffn[1], c, c + ADA_FIRST)
            with dve.Fori(ADA_ALL - ADA_FIRST, CH - 1) as c:
                ffn_dve(dve, ffn[1], c)
            ffn_dve(dve, ffn[1], CH - 1, norm=ln[1])
            dve.wait_ge(ada_evac, 2 * ADA_ALL + 1)
            dve.wait_ge(ffn[1].y_evac, UNIT_D * CH + 3)
            samples_in(dve)
            dve.sem_inc(resid_done, 1)
            prep(dve, 3, 4, 0)
            prep_gate(dve, 5, 1.0)
            norm_dve(dve, ln[1])
            for g in range(NG):
                norm_y(dve, ln[1], g)
            dve.wait_ge(ln_y, ln[1].at(NG - 1))
            samp_dve_run(dve)
            dve.memset(BIAS16[HD:, :, 0:HD], NEG / SCALE)
            dve.memset(parts[0:HD, 0:1], 1.0)
            dve.memset(parts[0:HD, 1:2], 0.0)
            dve.memset(parts[HD:, 0:1], 0.0)
            dve.memset(parts[HD:, 1:2], 1.0).then_inc(parts_set, 1)
            dve.wait_ge(parts_set, 1)
            for x in range(2):
                max_dve(dve, Half("L", 0, 0).step(x))
            for phase in "LMN":
                drive(dve, lambda hf: attn_dve(dve, hf), phase)
            values_dve(dve, LAST)
            merge_a_dve(dve, LAST)
            with dve.Fori(0, KT // 2) as i:
                wout_dve(dve, i)
            dve.wait_ge(wout_evac, NG * KT + 6)
            samples_in(dve)
            dve.sem_inc(resid_done, 1)
            prep(dve, 6, 7, 1)
            prep_gate(dve, 8, 0.5)
            center(dve, ln[2], 0)
            norm_dve(dve, ln[2])
            ffn_dve(dve, ffn[2], 0, before=ln[2])
            with dve.Fori(1, CH - 1) as c:
                ffn_dve(dve, ffn[2], c)
            ffn_dve(dve, ffn[2], CH - 1, norm=ln[3])
            dve.wait_ge(ffn[2].y_evac, UNIT_D * CH + 3)
            samples_in(dve)
            dve.sem_inc(resid_done, 1)
            prep(dve, None, None, 2, last_norm=True)
            norm_dve(dve, ln[3])
            for b in range(TB + 1):
                out_half(dve, b, 0)

        @block.tensor
        def _(pe):
            for n in (1, 2):
                pe.sem_inc(ffn[n].up_done, 6)
                pe.sem_inc(ffn[n].down_done, UNIT_D)
            for s in (qk_done, t_done, pv_done):
                pe.sem_inc(s, 2)
            pe.sem_inc(ada_done, 1)
            pe.wait_ge(const_ready, 4)
            pe.wait_ge(rows_in, 80)
            nv = MT + 6 * KT
            pe.transpose(bank[0][:, 0:nv], VROW[:, :], ident[0:nv, 0:nv]).then_inc(setup_pe, 1)
            nc_ = NC1 * KT
            pe.transpose(bank[1][:, 0:nc_], CROW[:, :], ident[0:nc_, 0:nc_]).then_inc(setup_pe, 1)
            pe.wait_ge(x_in, 32)
            for u in range(XU):
                k, h = u // 2, u % 2
                if u >= 4:
                    pe.wait_ge(setup_act, 1 + u - 3)
                for b in range(4):
                    last = pe.transpose(bank[2 + u % 4][:, b * P:(b + 1) * P],
                                        XTOK[:, 4 * h + b, k * P:(k + 1) * P], ident[:, :])
                last.then_inc(setup_pe, 1)
            for k in range(KT):
                last = pe.transpose(bank[6][:, k * NS:(k + 1) * NS], XSMP[:, k * P:(k + 1) * P],
                                    ident[0:NS, 0:NS])
            last.then_inc(setup_pe, 1)
            pe.wait_ge(rel_x, 1)
            pe.wait_ge(setup_act, 1)
            for n in range(4 * NH):
                k, h = n // NH, n % NH
                if n >= 2:
                    pe.wait_ge(bias_ev, n - 1)
                pe.matmul(bank[n % 2][:, 0:EXT], RELX[:, h + (NH if k == 3 else 0), :], HOT[:, k, :],
                          start=True, stop=True).then_inc(bias_mm, 1)
            pe.wait_ge(setup_act, 1)
            with pe.Fori(0, ADA_FIRST) as m:
                ada_pe(pe, m)
                ada_turn_pe(pe, m)
            with pe.Fori(0, ADA_ALL - ADA_FIRST) as c:
                ffn_pe(pe, ffn[1], c, c + ADA_FIRST)
            with pe.Fori(ADA_ALL - ADA_FIRST, CH - 1) as c:
                ffn_pe(pe, ffn[1], c)
            ffn_pe(pe, ffn[1], CH - 1, norm=ln[1])
            norm_pe(pe, ln[1])
            lo = [ln[1].half_at(g, 1) for g in range(NG)]
            with pe.Fori(0, PT // 2) as i:
                pair_pe(pe, "proj", proj_done, proj_evac, i, lo, ln_lo)
            pe.wait_ge(proj_evac, NG * PT + 6)
            samp_rows_pe(pe)
            pe.wait_ge(samp_dve, samp_at["rows"])
            for n in range(2):
                spread_pe(pe, n)
            for b in range(TB):
                kv_pe(pe, b)
                if b + 2 < NS:
                    spread_pe(pe, b + 2)
            pe.wait_ge(kv_evac, 2 * TB)
            pe.wait_ge(q_copied, NS)
            samp_pe_run(pe)
            pe.wait_ge(samp_done, 1)
            for x in range(2):
                scores_pe(pe, Half("L", 0, 0).step(x))
            pe.wait_ge(ones_set, 1)
            pe.wait_ge(v16_in, 16 * 2 * TB)
            pe.wait_ge(v4_in, 16 * TB)
            for phase in "LMN":
                drive(pe, lambda hf: attn_pe(pe, hf), phase)
            values_pe(pe, LAST)
            mix_pe(pe, TB - 1)
            with pe.Fori(0, KT // 2) as i:
                pair_pe(pe, "wout", wout_done, wout_evac, i, MIX_READY, mix_split)
            norm_pe(pe, ln[2])
            with pe.Fori(0, CH - 1) as c:
                ffn_pe(pe, ffn[2], c)
            ffn_pe(pe, ffn[2], CH - 1, norm=ln[3])
            norm_pe(pe, ln[3])
            for b in range(TB + 1):
                cols = slice(b * P, (b + 1) * P) if b < TB else slice(TP, T)
                rows = P if b < TB else NS
                pe.wait_ge(ln_hi, ln[3].half_at(min((b * P + rows - 1) // TG, NG - 1), 1))
                if b >= 2:
                    pe.wait_ge(out_ready, b - 1)
                for k in range(KT):
                    last = pe.transpose(bank[OUT_BANKS[b % 2][k // 4]][0:rows, (k % 4) * P:(k % 4 + 1) * P],
                                        Y[:, k, cols], ident[:, :])
                last.then_inc(out_pe, 1)


def kernel(**inputs):
    import numpy as _np
    import concourse.bacc as _bacc
    from concourse import mybir as _mybir
    from concourse.bass_utils import run_bass_kernel_spmd as _run

    nc = _bacc.Bacc("TRN2", target_bir_lowering=False, num_devices=1, dynamic_dma_scratch_size=1024)
    arrays, io = {}, {}
    for name, a in list(inputs.items()) + list(constants().items()):
        a = _np.ascontiguousarray(a)
        arrays[f"in_{name}"] = a
        io[name] = nc.dram_tensor(f"in_{name}", a.shape, _mybir.dt.from_np(a.dtype), kind="ExternalInput").ap()
    for name, shape in OUTPUTS:
        io[name] = nc.dram_tensor(f"out_{name}", shape, _mybir.dt.float32, kind="ExternalOutput").ap()
    build(nc, io)
    r = _run(nc, [arrays], core_ids=[0])
    return tuple(r.results[0][f"out_{name}"] for name, _ in OUTPUTS)
```
